# Optimizing a Trainium2 kernel written in Bass

```python
import math
import jax, jax.numpy as jnp
from jax import lax
import numpy as np

D_MODEL = 2048
BATCH = 1
SEQ = 256
DEPTH = 1

CHUNK = 64
D_MIX = D_MODEL
HEAD_DIM = 128
D_A = D_MIX // 2
D_B = D_MIX - D_A
H_A = D_A // HEAD_DIM
H_B = D_B // HEAD_DIM
LEFT_CHUNKS = 8
BAND = (LEFT_CHUNKS + 1) * CHUNK
MAX_REL = 128
IDX_H = 16
IDX_D = 64
TOPK_MAX = 256
Q_BLOCK = 128
EPS = 1e-6
SPLIT_SIZES = [D_A, D_A, D_A, D_A, D_B, D_B, D_B, D_B, IDX_H * IDX_D, IDX_D, IDX_H]
D_IN = sum(SPLIT_SIZES)

kernel_name = "hybrid_chunked_relpos_dsa_block"

def rms_norm(x, g):
    xf = x.astype(jnp.float32)
    y = xf * lax.rsqrt(jnp.mean(xf * xf, axis=-1, keepdims=True) + EPS)
    return (y * g.astype(jnp.float32)).astype(x.dtype)

def alibi_slopes(n_heads):
    return jnp.asarray([2.0 ** (-8.0 * (h + 1) / n_heads) for h in range(n_heads)], dtype=jnp.float32)

def chunked_relpos_attention(q, k, v, rel_bias):
    B, T, H, Dh = q.shape
    nc = T // CHUNK
    pad = LEFT_CHUNKS * CHUNK
    qc = q.reshape(B, nc, CHUNK, H, Dh)
    kp = jnp.pad(k, ((0, 0), (pad, 0), (0, 0), (0, 0)))
    vp = jnp.pad(v, ((0, 0), (pad, 0), (0, 0), (0, 0)))
    band = jnp.arange(nc)[:, None] * CHUNK + jnp.arange(BAND)[None, :]
    kb = kp[:, band]
    vb = vp[:, band]
    key_pos = band - pad
    q_pos = jnp.arange(T).reshape(nc, CHUNK)
    valid = key_pos >= 0
    rel = jnp.clip(q_pos[:, :, None] - key_pos[:, None, :], -MAX_REL, MAX_REL) + MAX_REL
    bias = rel_bias.astype(jnp.float32)[:, rel]
    s = jnp.einsum('bcqhd,bckhd->bhcqk', qc, kb).astype(jnp.float32) * (Dh ** -0.5) + bias[None]
    s = jnp.where(valid[None, None, :, None, :], s, -jnp.inf)
    p = jax.nn.softmax(s, axis=-1).astype(v.dtype)
    o = jnp.einsum('bhcqk,bckhd->bcqhd', p, vb)
    return o.reshape(B, T, H, Dh)

def dsa_sparse_attention(q, k, v, q_idx, k_idx, w_idx, slopes):
    B, T, H, Dh = q.shape
    top = min(TOPK_MAX, T // 4)
    nb = T // Q_BLOCK
    key_chunk = jnp.arange(T) // CHUNK
    idx_scale = (IDX_H ** -0.5) * (IDX_D ** -0.5)
    gather = jax.vmap(lambda arr, ii: arr[ii])

    def block(i):
        start = i * Q_BLOCK
        qb = lax.dynamic_slice_in_dim(q, start, Q_BLOCK, axis=1)
        qib = lax.dynamic_slice_in_dim(q_idx, start, Q_BLOCK, axis=1)
        wib = lax.dynamic_slice_in_dim(w_idx, start, Q_BLOCK, axis=1)
        q_pos = start + jnp.arange(Q_BLOCK)
        logits = jnp.einsum('bqhd,bsd->bqhs', qib, k_idx).astype(jnp.float32)
        score = jnp.einsum('bqh,bqhs->bqs', wib.astype(jnp.float32) * idx_scale, jax.nn.relu(logits))
        admissible = key_chunk[None, :] <= (q_pos // CHUNK)[:, None]
        score = jnp.where(admissible[None], score, -jnp.inf)
        sel_score, sel = lax.top_k(score, top)
        sel_valid = jnp.isfinite(sel_score)
        kg = gather(k, sel)
        vg = gather(v, sel)
        s = jnp.einsum('bqhd,bqjhd->bhqj', qb, kg).astype(jnp.float32) * (Dh ** -0.5)
        dist = jnp.abs(q_pos[None, :, None] - sel).astype(jnp.float32)
        s = s - slopes[None, :, None, None] * dist[:, None]
        s = jnp.where(sel_valid[:, None], s, -jnp.inf)
        p = jax.nn.softmax(s, axis=-1).astype(v.dtype)
        return jnp.einsum('bhqj,bqjhd->bqhd', p, vg)

    out = lax.map(block, jnp.arange(nb))
    return jnp.transpose(out, (1, 0, 2, 3, 4)).reshape(B, T, H, Dh)

def setup_inputs(seed: int = 0) -> dict:
    key = jax.random.key(seed)
    kx, kg, kin, krb, kout, kf = jax.random.split(key, 6)
    x = jax.random.normal(kx, (BATCH, SEQ, D_MODEL), jnp.float32)
    norm_gain = 1.0 + 0.01 * jax.random.normal(kg, (DEPTH, D_MODEL), jnp.float32)
    w_in = jax.random.normal(kin, (DEPTH, D_MODEL, D_IN), jnp.float32) * (D_MODEL ** -0.5)
    rel_bias = 0.5 * jax.random.normal(krb, (DEPTH, H_A, 2 * MAX_REL + 1), jnp.float32)
    w_out = jax.random.normal(kout, (DEPTH, D_MIX, D_MODEL), jnp.float32) * (D_MIX ** -0.5)
    final_gain = 1.0 + 0.01 * jax.random.normal(kf, (D_MODEL,), jnp.float32)
    return {"x": x, "norm_gain": norm_gain, "w_in": w_in, "rel_bias": rel_bias,
            "w_out": w_out, "final_gain": final_gain}

def reference(x, norm_gain, w_in, rel_bias, w_out, final_gain):
    B, T, _ = x.shape
    offsets = [int(o) for o in np.cumsum(SPLIT_SIZES)[:-1]]
    slopes = alibi_slopes(H_B)
    for l in range(DEPTH):
        h = rms_norm(x, norm_gain[l])
        proj = jnp.einsum('btd,de->bte', h, w_in[l])
        qa, ka, va, ga, qb, kb, vb, gb, qi, ki, wi = jnp.split(proj, offsets, axis=-1)
        heads = lambda t, n: t.reshape(B, T, n, HEAD_DIM)
        out_a = chunked_relpos_attention(heads(qa, H_A), heads(ka, H_A), heads(va, H_A), rel_bias[l])
        out_b = dsa_sparse_attention(heads(qb, H_B), heads(kb, H_B), heads(vb, H_B),
                                     qi.reshape(B, T, IDX_H, IDX_D), ki, wi, slopes)
        ya = out_a.reshape(B, T, D_A) * jax.nn.silu(ga)
        yb = out_b.reshape(B, T, D_B) * jax.nn.silu(gb)
        y = jnp.concatenate([ya, yb], axis=-1)
        x = x + jnp.einsum('bte,ed->btd', y, w_out[l])
    return rms_norm(x, final_gain)


_drawn_inputs = setup_inputs


def setup_inputs(seed=0):
    import zlib

    import numpy as np

    out = dict(_drawn_inputs(seed))
    spreads = {}
    factors = {}
    for name, (base, spread) in spreads.items():
        noise = np.random.default_rng([zlib.crc32(name.encode()), seed]).standard_normal(out[name].shape)
        drawn = base * np.exp(spread * noise) if base else spread * noise
        out[name] = __import__('jax').numpy.asarray(drawn.astype(out[name].dtype))
    for name, factor in factors.items():
        out[name] = (out[name] * factor).astype(out[name].dtype)
    return out
```

```python
"""Hybrid chunk-causal block on one core: RMSNorm, one input projection, chunked attention with a
relative bias (mixer A), top-k sparse attention with ALiBi (mixer B), gates, output projection,
residual and final RMSNorm.

Float32 products of the projections: both operands are split exactly into a high part (float32r, 12
significant bits, as the array takes them in one pass) and the rest (also exact in float32r); three
passes carry hi*hi, hi*lo and lo*hi, and lo*lo lies below the rounding of float32.
"""
"""Hybrid chunk-causal block on one core: RMSNorm, one input projection, chunked attention with a
relative bias (mixer A), top-k sparse attention with ALiBi (mixer B), gates, output projection,
residual and final RMSNorm.

Float32 products of the projections: both operands are split exactly into a high part (float32r, 12
significant bits, as the array takes them in one pass) and the rest (also exact in float32r); three
passes carry hi*hi, hi*lo and lo*hi, and lo*lo lies below the rounding of float32.
"""
"""Hybrid chunk-causal block on one core: RMSNorm, one input projection, chunked attention with a
relative bias (mixer A), top-k sparse attention with ALiBi (mixer B), gates, output projection,
residual and final RMSNorm.

Float32 products of the projections: both operands are split exactly into a high part (float32r, 12
significant bits, as the array takes them in one pass) and the rest (also exact in float32r); three
passes carry hi*hi, hi*lo and lo*hi, and lo*lo lies below the rounding of float32.
"""
"""Hybrid chunk-causal block on one core: RMSNorm, one input projection, chunked attention with a
relative bias (mixer A), top-k sparse attention with ALiBi (mixer B), gates, output projection,
residual and final RMSNorm.

Float32 products of the projections: both operands are split exactly into a high part (float32r, 12
significant bits, as the array takes them in one pass) and the rest (also exact in float32r); three
passes carry hi*hi, hi*lo and lo*hi, and lo*lo lies below the rounding of float32.
"""
"""Hybrid chunk-causal block on one core: RMSNorm, one input projection, chunked attention with a
relative bias (mixer A), top-k sparse attention with ALiBi (mixer B), gates, output projection,
residual and final RMSNorm.

Float32 products of the projections: both operands are split exactly into a high part (float32r, 12
significant bits, as the array takes them in one pass) and the rest (also exact in float32r); three
passes carry hi*hi, hi*lo and lo*hi, and lo*lo lies below the rounding of float32.
"""
"""Hybrid chunk-causal block on one core: RMSNorm, one input projection, chunked attention with a
relative bias (mixer A), top-k sparse attention with ALiBi (mixer B), gates, output projection,
residual and final RMSNorm.

Float32 products of the projections: both operands are split exactly into a high part (float32r, 12
significant bits, as the array takes them in one pass) and the rest (also exact in float32r); three
passes carry hi*hi, hi*lo and lo*hi, and lo*lo lies below the rounding of float32.
"""
"""Hybrid chunk-causal block on one core: RMSNorm, one input projection, chunked attention with a
relative bias (mixer A), top-k sparse attention with ALiBi (mixer B), gates, output projection,
residual and final RMSNorm.

Float32 products of the projections: both operands are split exactly into a high part (float32r, 12
significant bits, as the array takes them in one pass) and the rest (also exact in float32r); three
passes carry hi*hi, hi*lo and lo*hi, and lo*lo lies below the rounding of float32.
"""
"""Hybrid chunk-causal block on one core: RMSNorm, one input projection, chunked attention with a
relative bias (mixer A), top-k sparse attention with ALiBi (mixer B), gates, output projection,
residual and final RMSNorm.

Float32 products of the projections: both operands are split exactly into a high part (float32r, 12
significant bits, as the array takes them in one pass) and the rest (also exact in float32r); three
passes carry hi*hi, hi*lo and lo*hi, and lo*lo lies below the rounding of float32.
"""
"""Hybrid chunk-causal block on one core: RMSNorm, one input projection, chunked attention with a
relative bias (mixer A), top-k sparse attention with ALiBi (mixer B), gates, output projection,
residual and final RMSNorm.

Float32 products of the projections: both operands are split exactly into a high part (float32r, 12
significant bits, as the array takes them in one pass) and the rest (also exact in float32r); three
passes carry hi*hi, hi*lo and lo*hi, and lo*lo lies below the rounding of float32.
"""
import concourse.bass as bass
from concourse import mybir
from contextlib import ExitStack

P = 128
D = 2048
T = 256
TM = T // P
KT = D // P
CB = 512
HD = 128
HEADS = 8
CHUNK = 64
MAX_REL = 128
IDX_H, IDX_D = 16, 64
TOP = 64
EPS = 1e-6
NARROW = IDX_D + IDX_H
QK_SCALE = HD ** -0.5
IDX_SCALE = IDX_H ** -0.5 * IDX_D ** -0.5
BIG = 1e30
MASKED = -1e30
NOT_ADMITTED = -1e38
TAKEN = -3e38

G_QI, G_QB, G_KB, G_V, G_QKA, G_GATE, G_OUT, G_END = 0, 2, 4, 6, 10, 14, 18, 22
UK = 2
UNITS = KT // UK
RING = 4
AHEAD = RING


def hybrid_block(nc, xT, x, norm_gain, w_blocks, w_narrow, rel_bias, wo_blocks, final_gain, out):
    f32 = mybir.dt.float32
    f32r = mybir.dt.float32r
    ALU = mybir.AluOpType
    ACT = mybir.ActivationFunctionType
    AX = mybir.AxisListType
    ds = bass.ds

    with ExitStack() as ctx:
        def sb(name, shape, dt=f32):
            return ctx.enter_context(nc.sbuf_tensor(name, shape, dt))

        def pb(name, shape):
            return ctx.enter_context(nc.psum_tensor(name, shape, f32))

        def sem(name):
            return ctx.enter_context(nc.semaphore(name))

        w_raw = sb("w_raw", [P, RING, UK * CB])
        w_hi = sb("w_hi", [P, RING, UK, CB], f32r)
        w_lo = sb("w_lo", [P, RING, UK, CB], f32r)
        nw_raw = sb("nw_raw", [P, KT * NARROW])
        nw_hi = sb("nw_hi", [P, KT, NARROW], f32r)
        nw_lo = sb("nw_lo", [P, KT, NARROW], f32r)
        a_hi = sb("a_hi", [P, KT, T], f32r)
        a_lo = sb("a_lo", [P, KT, T], f32r)
        v = sb("v", [P, 4, TM, CB])
        x_nat = v[:, :, :, :].rearrange("p b m c -> p (b m c)").rearrange("p (m d) -> p m d", m=TM)
        o = sb("o", [P, 4, TM, CB])
        z_gain = o[:, :, :, :].rearrange("p b m c -> p (b m c)").rearrange("p (m d) -> p m d", m=TM)
        qk = sb("qk", [P, 8, 2 * T])
        qiT = sb("qiT", [P, 4, 2 * T])
        q_now = sb("q_now", [P, 2, T])
        stage = sb("stage", [P, TM, CB])
        ki_bd = sb("ki_bd", [P, 2, T])
        ki_nat = sb("ki_nat", [P, TM, P])
        narrow = sb("narrow", [NARROW, T])
        w_idx = sb("w_idx", [P, TM, IDX_H])
        relu1 = sb("relu1", [P, 2, T])
        relu0 = sb("relu0", [P, 2, P])
        iscore1 = sb("iscore1", [P, T])
        iscore0 = sb("iscore0", [P, P])
        top1 = sb("top1", [P, 8])
        top0 = sb("top0", [P, 8])
        carrier = sb("carrier", [P, 1])
        dist = sb("dist", [P, T])
        dist1 = sb("dist1", [P, T])
        dist0 = sb("dist0", [P, P])
        bias = sb("bias", [P, HEADS, T])
        bias_ext = sb("bias_ext", [HEADS, 3 * P])
        bias_row = sb("bias_row", [HEADS, 2 * MAX_REL + 1])
        neg_slope = sb("neg_slope", [P, HEADS])
        qscale = sb("qscale", [P, 1])
        p1 = sb("p1", [P, 2, T])
        p0 = sb("p0", [P, 2, P])
        pT1 = sb("pT1", [P, 2, 2, P])
        pT0 = sb("pT0", [P, 2, P])
        neg_max = sb("neg_max", [P, 2, 2])
        p_sum = sb("p_sum", [P, 2, 2])
        p_inv = sb("p_inv", [P, 2, 2])
        t_gate = sb("t_gate", [P, TM, CB])
        z = sb("z", [P, TM, CB])
        ident = sb("ident", [P, P])
        gain = sb("gain", [P, KT])
        fgain = sb("fgain", [P, D])
        ssq = sb("ssq", [P, TM])
        rstd = sb("rstd", [P, TM])
        half_rstd = sb("half_rstd", [P, TM])
        zsq = sb("zsq", [P, TM, 4])
        zrstd = sb("zrstd", [P, TM])

        xT_land = qk[:, :, :].rearrange("p c t -> p (c t)").rearrange("p (k t) -> p k t", k=KT)

        acc = pb("acc", [P, 4 * CB])
        aux = [pb(f"aux{i}", [P, CB]) for i in range(4)]

        w_landed = [sem(f"w_landed{s}") for s in range(RING)]
        hi_done = sem("hi_done")
        lo_done = sem("lo_done")
        mm_done = sem("mm_done")
        x_landed = [sem(f"x_landed{c}") for c in range(2 * TM)]
        xT_landed = [sem(f"xT_landed{c}") for c in range(UNITS)]
        nw_landed = sem("nw_landed")
        gain_landed = sem("gain_landed")
        row_landed = sem("row_landed")
        fgain_landed = sem("fgain_landed")
        ext_ready = sem("ext_ready")
        ext_stored = sem("ext_stored")
        bias_landed = sem("bias_landed")
        res_landed = sem("res_landed")
        out_landed = sem("out_landed")
        cleared = sem("cleared")
        patterned = sem("patterned")
        eps_ready = sem("eps_ready")
        ahi_done = sem("ahi_done")
        alo_done = sem("alo_done")
        nhi_done = sem("nhi_done")
        nlo_done = sem("nlo_done")
        ssq_done = sem("ssq_done")
        var_done = sem("var_done")
        std_done = sem("std_done")
        rstd_done = sem("rstd_done")
        narrow_done = sem("narrow_done")
        kit_done = sem("kit_done")
        aux_read = [sem(f"aux{i}_read") for i in range(4)]
        acc_out = [sem("acc0_out"), sem("acc1_out")]
        tr_done = sem("tr_done")
        qnow_ready = sem("qnow_ready")
        iscored = sem("iscored")
        isum_done = sem("isum_done")
        isum_step = sem("isum_step")
        top_step = sem("top_step")
        pen_step = sem("pen_step")
        bias_masked = sem("bias_masked")
        scored = sem("scored")
        biased = sem("biased")
        max_done = sem("max_done")
        exp_done = sem("exp_done")
        inv_done = sem("inv_done")
        pt_done = sem("pt_done")
        pv_done = sem("pv_done")
        o_out = sem("o_out")
        tanh_done = sem("tanh_done")
        y_done = sem("y_done")
        ytr_done = sem("ytr_done")
        yhi_done = sem("yhi_done")
        ylo_done = sem("ylo_done")
        zsq_done = sem("zsq_done")
        zg_done = sem("zg_done")
        tail_done = sem("tail_done")
        fin_sum = sem("fin_sum")
        fin_std = sem("fin_std")
        fin_rstd = sem("fin_rstd")
        fin_ready = [sem("fin_ready0"), sem("fin_ready1")]

        bias_dram = nc.dram_tensor("bias_dram", (P, HEADS, T), f32, kind="Internal").ap()

        AUX01_INDEX, AUX01_PAIRS, AUX01_Y = 2, 10, 18
        AUX23_BLOCKS, AUX23_B, AUX23_A, AUX23_Y = 0, 6, 14, 18
        HALF = CHUNK

        def flat(t):
            return t.rearrange("p a b -> p (a b)")

        v_flat = v[:, :, :, :].rearrange("p b m c -> p (b m c)")
        o_flat = o[:, :, :, :].rearrange("p b m c -> p (b m c)")
        qnow_flat = flat(q_now[:, :, :])
        PAIR = 2 * HD
        VECTOR_QUARTERS = ((0, 0), (0, 1), (1, 0))

        def place(pair, m):
            return (pair // 2) * (TM * CB) + (pair % 2) * PAIR + m * CB

        block = ctx.enter_context(nc.Block())

        @block.sync
        def _(sp):
            def load(u, src):
                sp.dma_start(w_raw[:, u % RING, :], src).then_inc(w_landed[u % RING], 16)

            sp.dma_start(gain[:, :], norm_gain).then_inc(gain_landed, 16)
            for u in range(UNITS):
                k = slice(UK * u, UK * u + UK)
                sp.dma_start(xT_land[:, k, :], xT[:, k, :]).then_inc(xT_landed[u], 16)
                if u < RING:
                    load(u, w_blocks[0, u, :, :])
            for u in range(RING, UNITS):
                sp.wait_ge(lo_done, u - RING + 1)
                load(u, w_blocks[0, u, :, :])
                m, h = divmod(u - RING, 2)
                c = slice(h * (D // 2), (h + 1) * (D // 2))
                sp.dma_start(x_nat[:, m, c], x[:, m, c]).then_inc(x_landed[u - RING], 16)
            sp.dma_start(nw_raw[:, :], w_narrow).then_inc(nw_landed, 16)
            with sp.Fori(1, G_OUT) as g:
                for u in range(UNITS):
                    sp.wait_ge(lo_done, g * UNITS + (u - RING + 1))
                    load(u, w_blocks[ds(g, 1), u, :, :].rearrange("o p c -> (o p) c"))
            with sp.Fori(G_OUT, G_END) as g:
                for u in range(UNITS):
                    sp.wait_ge(lo_done, g * UNITS + (u - RING + 1))
                    load(u, wo_blocks[ds(g - G_OUT, 1), u, :, :].rearrange("o p c -> (o p) c"))
            for n, (m, h) in enumerate(VECTOR_QUARTERS):
                c = slice(h * (D // 2), (h + 1) * (D // 2))
                sp.wait_ge(fin_ready[1], n + 1)
                sp.dma_start(out[m * P:m * P + P, c], z_gain[:, m, c]).then_inc(out_landed, 16)
            sp.wait_ge(out_landed, 64)

        @block.gpsimd
        def _(pool):
            pool.dma_start(bias_row[:, :], rel_bias).then_inc(row_landed, 16)
            nc.gpsimd.memset(ident[:, :], 0.0).then_inc(cleared, 1)
            nc.gpsimd.memset(ki_bd[:, :, :], 0.0).then_inc(cleared, 1)
            nc.gpsimd.memset(qscale[:, :], QK_SCALE).then_inc(cleared, 1)
            for h in range(HEADS):
                nc.gpsimd.memset(neg_slope[:, h:h + 1], -(2.0 ** (-8.0 * (h + 1) / HEADS))).then_inc(cleared, 1)
            pool.wait_ge(cleared, 3 + HEADS)
            nc.gpsimd.affine_select(out=ident[:, :], in_=ident[:, :], compare_op=ALU.not_equal, fill=1.0,
                                    base=0, pattern=[[-1, P]], channel_multiplier=1).then_inc(patterned, 1)
            nc.gpsimd.iota(dist[:, :], pattern=[[-1, T]], base=P, channel_multiplier=1,
                           allow_small_or_imprecise_dtypes=True).then_inc(patterned, 1)
            pool.wait_ge(aux_read[2], AUX23_BLOCKS + 1)
            pool.wait_ge(aux_read[3], AUX23_BLOCKS + 1)
            nc.gpsimd.tensor_copy(qnow_flat, qiT[:, 0, :]).then_inc(qnow_ready, 1)
            with pool.Fori(1, 4) as i:
                pool.wait_ge(iscored, 2 * i)
                pool.wait_ge(aux_read[2], i // 2 + (AUX23_BLOCKS + 1))
                pool.wait_ge(aux_read[3], i // 2 + (AUX23_BLOCKS + 1))
                nc.gpsimd.tensor_copy(qnow_flat, flat(qiT[:, ds(i, 1), :])).then_inc(qnow_ready, 1)

            pool.wait_ge(ext_ready, 2)
            ext = bias_ext[:, :]
            windows = bass.AP(tensor=ext.tensor, offset=ext.offset + P - 1, ap=[list(ext.ap[0]), [-1, P], [1, T]])
            pool.dma_start(bias_dram.rearrange("p h c -> h p c"), windows).then_inc(ext_stored, 16)
            pool.wait_ge(ext_stored, 16)
            pool.dma_start(bias[:, :, :], bias_dram).then_inc(bias_landed, 16)
            pool.dma_start(fgain[:, :], final_gain.partition_broadcast(P)).then_inc(fgain_landed, 16)

            def scaled(chunk):
                nc.gpsimd.tensor_tensor(qnow_flat, flat(qk[:, ds(chunk, 1), :]),
                                        qscale[:, :].broadcast_to((P, 2 * T)), ALU.mult).then_inc(qnow_ready, 1)

            pool.wait_ge(iscored, 2 * 4)
            pool.wait_ge(aux_read[2], AUX23_B)
            pool.wait_ge(aux_read[3], AUX23_B)
            scaled(0)
            with pool.Fori(1, 4) as i:
                pool.wait_ge(scored, i)
                scaled(2 * i)
            with pool.Fori(0, 4) as i:
                pool.wait_ge(scored, i + 4)
                pool.wait_ge(aux_read[2], (i // 2) * 2 + (AUX23_B + 2))
                pool.wait_ge(aux_read[3], (i // 2) * 2 + (AUX23_B + 2))
                scaled(i)
            pool.wait_ge(pv_done, HEADS)
            pool.dma_start(x_nat, x).then_inc(res_landed, 16)

        @block.tensor
        def _(pe):
            def mm3(dst, k, m, hi, lo, start, stop):
                t = slice(m * P, m * P + P)
                nc.tensor.matmul(dst, a_hi[:, k, t], hi, start=start, stop=False)
                nc.tensor.matmul(dst, a_hi[:, k, t], lo, start=False, stop=False)
                return nc.tensor.matmul(dst, a_lo[:, k, t], hi, start=False, stop=stop)

            def unit(g, u):
                if u == 0 and not (isinstance(g, int) and g < 2):
                    pe.wait_ge(acc_out[0], g - 1)
                    pe.wait_ge(acc_out[1], g - 1)
                pe.wait_ge(lo_done, g * UNITS + (u + 1))
                for kk in range(UK):
                    k = u * UK + kk
                    for m in range(TM):
                        dst = acc[:, ds((g % 2) * (TM * CB) + m * CB, CB)]
                        last = mm3(dst, k, m, w_hi[:, u % RING, kk, :], w_lo[:, u % RING, kk, :],
                                   k == 0, k == KT - 1)
                last.then_inc(mm_done, 1)

            def transposes(tb, g, used):
                pe.wait_ge(acc_out[0], g + 1)
                pe.wait_ge(acc_out[1], g + 1)
                for half in range(2):
                    if used is not None:
                        pe.wait_ge(aux_read[2 + half], used)
                    for h in range(2):
                        for m in range(TM):
                            c = (2 * half + h) * HD
                            last = nc.tensor.transpose(aux[2 + half][:, h * T + m * P:h * T + m * P + P],
                                                       stage[:, m, c:c + HD], ident[:, :])
                    last.then_inc(tr_done, 1)

            for u in range(UNITS):
                pe.wait_ge(alo_done, UK * u + UK)
                unit(0, u)
            for u in range(4):
                unit(1, u)
            pe.wait_ge(patterned, 1)
            transposes(0, 0, None)
            unit(1, 4)
            unit(1, 5)

            pe.wait_ge(nlo_done, 1)
            for k in range(KT):
                for n, (w, a) in enumerate(((nw_hi, a_hi), (nw_hi, a_lo), (nw_lo, a_hi))):
                    last = nc.tensor.matmul(aux[0][0:NARROW, 0:T], w[:, k, :], a[:, k, :],
                                            start=(k == 0 and n == 0), stop=(k == KT - 1 and n == 2))
            last.then_inc(narrow_done, 1)
            unit(1, 6)
            unit(1, 7)
            pe.wait_ge(aux_read[0], 1)
            for m in range(TM):
                last = nc.tensor.transpose(aux[1][:, m * P:m * P + NARROW], narrow[:, m * P:m * P + P],
                                           ident[0:NARROW, 0:NARROW])
            last.then_inc(narrow_done, 1)
            unit(2, 0)
            pe.wait_ge(aux_read[1], 2)
            for m in range(TM):
                last = nc.tensor.transpose(aux[0][:, m * P:m * P + P], ki_nat[:, m, :], ident[:, :])
            last.then_inc(kit_done, 1)
            unit(2, 1)
            transposes(1, 1, 1)

            with pe.Fori(0, 4) as i:
                g = i + G_QB

                def index_pair(c):
                    pe.wait_ge(qnow_ready, i + 1)
                    pe.wait_ge(aux_read[0], 2 * i + (AUX01_INDEX + c))
                    pe.wait_ge(aux_read[1], 2 * i + (AUX01_INDEX + c))
                    nc.tensor.matmul(aux[0][:, :], q_now[:, c, P:T], ki_bd[:, :, :], start=True, stop=True)
                    nc.tensor.matmul(aux[1][:, 0:2 * P], q_now[:, c, 0:P], ki_bd[:, :, 0:P],
                                     start=True, stop=True).then_inc(iscored, 1)

                unit(g, 2)
                index_pair(0)
                unit(g, 3)
                unit(g, 4)
                index_pair(1)
                for u in range(5, UNITS):
                    unit(g, u)
                unit(g + 1, 0)
                unit(g + 1, 1)
                transposes(g, g, i + (AUX23_BLOCKS + G_QB))

            with pe.Fori(G_V, G_QKA) as g:
                for u in range(2, UNITS):
                    unit(g, u)
                unit(g + 1, 0)
                unit(g + 1, 1)

            def score_pair(pair, k_chunk):
                pe.wait_ge(qnow_ready, pair + 5)
                pe.wait_ge(aux_read[0], pair + AUX01_PAIRS)
                pe.wait_ge(aux_read[1], pair + AUX01_PAIRS)
                for h in range(2):
                    nc.tensor.matmul(aux[0][:, h * T:h * T + T], q_now[:, h, P:T],
                                     flat(qk[:, ds(k_chunk, 1), h * T:h * T + T]), start=True, stop=True)
                for h in range(2):
                    last = nc.tensor.matmul(aux[1][:, h * P:h * P + P], q_now[:, h, 0:P],
                                            flat(qk[:, ds(k_chunk, 1), h * T:h * T + P]), start=True, stop=True)
                last.then_inc(scored, 1)

            def transpose_pair(pair, used2):
                pe.wait_ge(exp_done, pair + 1)
                pe.wait_ge(aux_read[2], used2)
                for h in range(2):
                    for kt in range(TM):
                        c = (2 * h + kt) * P
                        nc.tensor.transpose(aux[2][:, c:c + P], p1[:, h, kt * P:kt * P + P], ident[:, :])
                for h in range(2):
                    last = nc.tensor.transpose(aux[1][:, h * P:h * P + P], p0[:, h, :], ident[:, :])
                last.then_inc(pt_done, 1)

            def value_pair(pair, used2, used3):
                pe.wait_ge(aux_read[2], used2 + 1)
                pe.wait_ge(aux_read[1], pair + (AUX01_PAIRS + 1))
                pe.wait_ge(aux_read[3], used3)
                for h in range(2):
                    for kt in range(TM):
                        nc.tensor.matmul(aux[3][:, h * HD:h * HD + HD], pT1[:, h, kt, :],
                                         v_flat[:, ds(place(pair, kt) + h * HD, HD)],
                                         start=(kt == 0), stop=(kt == TM - 1))
                for h in range(2):
                    last = nc.tensor.matmul(aux[3][:, (2 + h) * HD:(3 + h) * HD], pT0[:, h, :],
                                            v_flat[:, ds(place(pair, 0) + h * HD, HD)], start=True, stop=True)
                last.then_inc(pv_done, 1)

            with pe.Fori(0, 4) as i:
                g = i + G_QKA
                used = 2 * i + AUX23_B
                unit(g, 2)
                score_pair(i, 2 * i + 1)
                for u in (3, 4, 5):
                    unit(g, u)
                transpose_pair(i, used)
                unit(g, 6)
                value_pair(i, used, used)
                unit(g, 7)
                unit(g + 1, 0)
                unit(g + 1, 1)
                transposes(None, g, used + 1)

            def gate_block(g, i):
                used = i + AUX23_A
                unit(g, 2)
                pe.wait_ge(aux_read[2], (i // 2) * 2 + (AUX23_B + 6))
                pe.wait_ge(aux_read[3], (i // 2) * 2 + (AUX23_B + 6))
                score_pair(i + 4, i + 4)
                for u in (3, 4, 5):
                    unit(g, u)
                transpose_pair(i + 4, used)
                unit(g, 6)
                value_pair(i + 4, used, used)
                unit(g, 7)

            with pe.Fori(0, 3) as i:
                gate_block(i + G_GATE, i)
                unit(i + (G_GATE + 1), 0)
                unit(i + (G_GATE + 1), 1)
            gate_block(G_OUT - 1, 3)

            def y_transposes(q):
                pe.wait_ge(y_done, 2 * (q // 2) + 2)
                if q < 4:
                    pe.wait_ge(aux_read[q], AUX01_Y if q < 2 else AUX23_Y)
                else:
                    pe.wait_ge(ylo_done, q - 3)
                for kk in range(UK):
                    for m in range(TM):
                        c = (q % 2) * PAIR + kk * HD
                        last = nc.tensor.transpose(aux[q % 4][:, kk * T + m * P:kk * T + m * P + P],
                                                   o[:, q // 2, m, c:c + HD], ident[:, :])
                last.then_inc(ytr_done, 1)

            for q in range(4):
                y_transposes(q)
            for u in range(UNITS):
                pe.wait_ge(ylo_done, u + 1)
                unit(G_OUT, u)
                if u < 4:
                    y_transposes(u + 4)
            with pe.Fori(G_OUT + 1, G_END - 1) as g:
                for u in range(UNITS):
                    unit(g, u)
            g = G_END - 1
            for u in range(UNITS - RING):
                unit(g, u)
            for m in range(TM):
                for u in range(UNITS - RING, UNITS):
                    pe.wait_ge(lo_done, g * UNITS + (u + 1))
                    for kk in range(UK):
                        k = u * UK + kk
                        bank = ((g % 2) * TM + m) * CB
                        last = mm3(acc[:, bank:bank + CB], k, m, w_hi[:, u % RING, kk, :], w_lo[:, u % RING, kk, :],
                                   False, k == KT - 1)
                last.then_inc(tail_done, 1)

        @block.scalar
        def _(act):
            def split_hi(g, c):
                u = c % UNITS
                s = u % RING
                act.wait_ge(w_landed[s], g * (16 * UNITS // RING) + 16 * (c // RING + 1))
                if not (isinstance(g, int) and g * UNITS + c < RING):
                    act.wait_ge(mm_done, g * UNITS + (c - RING + 1))
                nc.scalar.activation(flat(w_hi[:, s, :, :]), w_raw[:, s, :], ACT.Copy).then_inc(hi_done, 1)

            def block_out(g, dst, tr=None):
                act.wait_ge(mm_done, g * UNITS + UNITS)
                if tr is not None:
                    act.wait_ge(tr_done, tr)
                nc.scalar.activation(dst, acc[:, ds((g % 2) * (TM * CB), CB)], ACT.Copy,
                                     scale=rstd[:, 0:1]).then_inc(acc_out[0], 1)

            def first_half_out(tb, dst):
                act.wait_ge(tr_done, 2 * tb + 1)
                nc.scalar.activation(dst, aux[2][:, :], ACT.Copy).then_inc(aux_read[2], 1)

            nc.scalar.preload_act_table(ACT.Exp)
            act.wait_ge(gain_landed, 16)
            for u in range(UNITS):
                act.wait_ge(xT_landed[u], 16)
                for k in range(UK * u, UK * u + UK):
                    nc.scalar.activation(a_hi[:, k, :], xT_land[:, k, :], ACT.Copy,
                                         scale=gain[:, k:k + 1]).then_inc(ahi_done, 1)
                split_hi(0, u)
            nc.scalar.preload_act_table(ACT.Sqrt)
            split_hi(0, 8)
            for m in range(TM):
                act.wait_ge(x_landed[2 * m], 16)
                act.wait_ge(x_landed[2 * m + 1], 16)
                nc.scalar.activation(o_flat[:, m * D:m * D + D], x_nat[:, m, :], ACT.Square,
                                     accum_out=ssq[:, m:m + 1]).then_inc(ssq_done, 1)
                split_hi(0, 9 + m)
            act.wait_ge(var_done, 1)
            nc.scalar.activation(rstd[:, :], ssq[:, :], ACT.Sqrt).then_inc(std_done, 1)
            nc.scalar.preload_act_table(ACT.Exp)
            act.wait_ge(nw_landed, 16)
            nc.scalar.activation(flat(nw_hi[:, :, :]), nw_raw[:, :], ACT.Copy).then_inc(nhi_done, 1)
            for c in (11, 12, 13):
                split_hi(0, c)
            act.wait_ge(rstd_done, 2)
            block_out(0, stage[:, 0, :])
            split_hi(0, 14)
            split_hi(0, 15)
            first_half_out(0, qiT[:, 0, :])
            split_hi(0, 16)
            split_hi(0, 17)
            act.wait_ge(narrow_done, 1)
            nc.scalar.activation(narrow[:, :], aux[0][0:NARROW, 0:T], ACT.Copy).then_inc(aux_read[0], 1)
            split_hi(0, 18)
            split_hi(0, 19)
            block_out(1, stage[:, 0, :], 2)
            split_hi(0, 20)
            split_hi(0, 21)
            first_half_out(1, qiT[:, 2, :])

            with act.Fori(0, 4) as i:
                g = i + G_QB

                def index_relu(c):
                    act.wait_ge(iscored, 2 * i + (c + 1))
                    act.wait_ge(isum_done, 2 * i + (c + 1))
                    nc.scalar.activation(flat(relu1[:, :, :]), aux[0][:, :], ACT.Relu).then_inc(aux_read[0], 1)
                    nc.scalar.activation(flat(relu0[:, :, :]), aux[1][:, 0:2 * P],
                                         ACT.Relu).then_inc(aux_read[1], 1)

                split_hi(g, 6)
                index_relu(0)
                split_hi(g, 7)
                split_hi(g, 8)
                index_relu(1)
                for c in (9, 10, 11):
                    split_hi(g, c)
                block_out(g, stage[:, 0, :], 2 * i + 2 * G_QB)
                split_hi(g, 12)
                split_hi(g, 13)
                first_half_out(g, flat(qk[:, ds((i % 2) * 4 + i // 2, 1), :]))

            with act.Fori(0, 4) as i:
                g = i + G_V
                for c in range(6, 12):
                    split_hi(g, c)
                block_out(g, v_flat[:, ds(i * (TM * CB), CB)])
                split_hi(g, 12)
                split_hi(g, 13)

            def exps(pair):
                for t, p in enumerate((p1, p0)):
                    act.wait_ge(max_done, 2 * pair + (t + 1))
                    for h in range(2):
                        last = nc.scalar.activation(p[:, h, :], p[:, h, :], ACT.Exp, bias=neg_max[:, t, h:h + 1],
                                                    accum_out=p_sum[:, t, h:h + 1])
                last.then_inc(exp_done, 1)

            def pT0_out(pair):
                act.wait_ge(pt_done, pair + 1)
                nc.scalar.activation(flat(pT0[:, :, :]), aux[1][:, 0:2 * P], ACT.Copy).then_inc(aux_read[1], 1)

            with act.Fori(0, 4) as i:
                g = i + G_QKA
                split_hi(g, 6)
                split_hi(g, 7)
                exps(i)
                split_hi(g, 8)
                split_hi(g, 9)
                pT0_out(i)
                split_hi(g, 10)
                split_hi(g, 11)
                block_out(g, stage[:, 0, :], 2 * i + 2 * G_V)
                split_hi(g, 12)
                split_hi(g, 13)
                first_half_out(i + G_V, flat(qk[:, ds(2 * i, 1), :]))

            def gate_block(g, i):
                split_hi(g, 6)
                split_hi(g, 7)
                exps(i + 4)
                split_hi(g, 8)
                split_hi(g, 9)
                pT0_out(i + 4)
                split_hi(g, 10)

            def tanh_gate(g, m):
                act.wait_ge(mm_done, g * UNITS + UNITS)
                nc.scalar.activation(t_gate[:, m, :], acc[:, ds((g % 2) * (TM * CB) + m * CB, CB)], ACT.Tanh,
                                     scale=half_rstd[:, m:m + 1]).then_inc(tanh_done, 1)

            with act.Fori(0, 3) as i:
                g = i + G_GATE
                gate_block(g, i)
                split_hi(g, 11)
                for m in range(TM):
                    tanh_gate(g, m)
                split_hi(g, 12)
                split_hi(g, 13)
            gate_block(G_OUT - 1, 3)

            def y_hi(q):
                act.wait_ge(ytr_done, q + 1)
                nc.scalar.activation(flat(a_hi[:, UK * q:UK * q + UK, :]), aux[q % 4][:, :],
                                     ACT.Copy).then_inc(yhi_done, 1)

            act.wait_ge(mm_done, G_OUT * UNITS)
            y_hi(0)
            tanh_gate(G_OUT - 1, 0)
            y_hi(1)
            tanh_gate(G_OUT - 1, 1)
            split_hi(G_OUT, 3)
            y_hi(2)
            y_hi(3)
            for q in range(4, 8):
                y_hi(q)
                split_hi(G_OUT, q)

            nc.scalar.preload_act_table(ACT.Sqrt)

            def square(b, m):
                act.wait_ge(acc_out[m], b + (G_OUT + 1))
                nc.scalar.activation(t_gate[:, m, :], z[:, m, :], ACT.Square,
                                     accum_out=zsq[:, m, ds(b, 1)]).then_inc(zsq_done, 1)

            for c in range(8, 12):
                split_hi(G_OUT, c)
            square(0, 0)
            square(0, 1)
            with act.Fori(1, 3) as b:
                for c in range(4, 12):
                    split_hi(b + G_OUT, c)
                square(b, 0)
                square(b, 1)
            for c in range(4, 8):
                split_hi(G_END - 1, c)
            for m in range(TM):
                square(3, m)
                act.wait_ge(var_done, 2 + m)
                nc.scalar.activation(zrstd[:, m:m + 1], zrstd[:, m:m + 1], ACT.Sqrt).then_inc(fin_std, 1)
            act.wait_ge(fin_rstd, 2)
            nc.scalar.activation(z_gain[:, 1, D // 2:D], z_gain[:, 1, D // 2:D], ACT.Copy,
                                 scale=zrstd[:, 1:2]).then_inc(fin_ready[0], 1)
            act.wait_ge(fin_ready[0], 1)
            act.dma_start(out[P:2 * P, D // 2:D], z_gain[:, 1, D // 2:D]).then_inc(out_landed, 16)

        @block.vector
        def _(dve):
            def split_lo(g, c):
                s = c % RING
                dve.wait_ge(hi_done, g * UNITS + (c + 1))
                nc.vector.tensor_tensor(flat(w_lo[:, s, :, :]), w_raw[:, s, :], flat(w_hi[:, s, :, :]).bitcast(f32),
                                        ALU.subtract).then_inc(lo_done, 1)

            def block_out(g, dst, tr=None):
                dve.wait_ge(mm_done, g * UNITS + UNITS)
                if tr is not None:
                    dve.wait_ge(tr_done, tr)
                nc.vector.tensor_scalar(dst, acc[:, ds((g % 2) * (TM * CB) + CB, CB)], rstd[:, 1:2], None,
                                        ALU.mult).then_inc(acc_out[1], 1)

            def second_half_out(tb, dst):
                dve.wait_ge(tr_done, 2 * tb + 2)
                nc.vector.tensor_copy(dst, aux[3][:, :]).then_inc(aux_read[3], 1)

            dve.wait_ge(row_landed, 16)
            nc.vector.tensor_copy(bias_ext[:, 0:P - 1],
                                  bias_row[:, 2 * MAX_REL:2 * MAX_REL + 1].broadcast_to((HEADS, P - 1))).then_inc(ext_ready, 1)
            nc.vector.tensor_copy(bias_ext[:, P - 1:3 * P], bias_row[:, ::-1]).then_inc(ext_ready, 1)

            dve.wait_ge(gain_landed, 16)
            for u in range(UNITS):
                for k in range(UK * u, UK * u + UK):
                    dve.wait_ge(ahi_done, k + 1)
                    nc.vector.scalar_tensor_tensor(a_lo[:, k, :], xT_land[:, k, :], gain[:, k:k + 1],
                                                   a_hi[:, k, :].bitcast(f32), ALU.mult,
                                                   ALU.subtract).then_inc(alo_done, 1)
                split_lo(0, u)
            nc.vector.memset(iscore1[:, :], 0.0)
            nc.vector.memset(iscore0[:, :], 0.0).then_inc(isum_done, 1)
            dve.wait_ge(patterned, 2)
            nc.vector.scalar_tensor_tensor(dist[:, :], dist[:, :], -1.0, dist[:, :], ALU.mult,
                                           ALU.max).then_inc(pen_step, 1)
            for c in (8, 9, 10):
                split_lo(0, c)
            dve.wait_ge(ssq_done, TM)
            nc.vector.tensor_scalar(ssq[:, :], ssq[:, :], 1.0 / D, EPS, ALU.mult, ALU.add).then_inc(var_done, 1)
            dve.wait_ge(std_done, 1)
            nc.vector.reciprocal(rstd[:, :], rstd[:, :]).then_inc(rstd_done, 1)
            dve.wait_ge(rstd_done, 1)
            nc.vector.tensor_scalar(half_rstd[:, :], rstd[:, :], 0.5, None, ALU.mult).then_inc(rstd_done, 1)
            dve.wait_ge(nhi_done, 1)
            nc.vector.tensor_tensor(flat(nw_lo[:, :, :]), nw_raw[:, :], flat(nw_hi[:, :, :]).bitcast(f32),
                                    ALU.subtract).then_inc(nlo_done, 1)
            for c in (11, 12, 13):
                split_lo(0, c)
            block_out(0, stage[:, 1, :])
            split_lo(0, 14)
            split_lo(0, 15)
            second_half_out(0, qiT[:, 1, :])
            for c in (16, 17, 18, 19):
                split_lo(0, c)
            block_out(1, stage[:, 1, :], 2)
            dve.wait_ge(narrow_done, 2)
            for m in range(TM):
                for h in range(2):
                    nc.vector.tensor_scalar(ki_nat[:, m, h * IDX_D:(h + 1) * IDX_D],
                                            aux[1][:, m * P:m * P + IDX_D], rstd[:, m:m + 1], None, ALU.mult)
                nc.vector.tensor_scalar(w_idx[:, m, :], aux[1][:, m * P + IDX_D:m * P + NARROW], rstd[:, m:m + 1],
                                        IDX_SCALE, ALU.mult, ALU.mult).then_inc(aux_read[1], 1)
            split_lo(0, 20)
            dve.wait_ge(kit_done, 1)
            dve.wait_ge(cleared, 2)
            nc.vector.tensor_copy(ki_bd[0:IDX_D, 0, :], aux[0][0:IDX_D, 0:T])
            nc.vector.tensor_copy(ki_bd[IDX_D:P, 1, :], aux[0][IDX_D:P, 0:T]).then_inc(aux_read[0], 1)
            split_lo(0, 21)
            second_half_out(1, qiT[:, 3, :])

            with dve.Fori(0, 4) as i:
                g = i + G_QB

                def index_sum(c):
                    dve.wait_ge(aux_read[0], 2 * i + (AUX01_INDEX + c + 1))
                    dve.wait_ge(aux_read[1], 2 * i + (AUX01_INDEX + c + 1))
                    dve.wait_ge(isum_done, 2 * i + (c + 1))
                    for h in range(2):
                        for t, (relu, total) in enumerate(((relu1, iscore1), (relu0, iscore0))):
                            if h == 1:
                                dve.wait_ge(isum_step, 4 * i + (2 * c + t + 1))
                            last = nc.vector.scalar_tensor_tensor(
                                total[:, :], relu[:, h, :], w_idx[:, 1 - t, ds(4 * i + (2 * c + h), 1)],
                                total[:, :], ALU.mult, ALU.add)
                            if h == 0:
                                last.then_inc(isum_step, 1)
                    last.then_inc(isum_done, 1)

                split_lo(g, 6)
                split_lo(g, 7)
                index_sum(0)
                split_lo(g, 8)
                split_lo(g, 9)
                index_sum(1)
                split_lo(g, 10)
                split_lo(g, 11)
                block_out(g, stage[:, 1, :], 2 * i + 2 * G_QB)
                split_lo(g, 12)
                split_lo(g, 13)
                second_half_out(g, flat(qk[:, ds((i % 2) * 4 + i // 2 + 2, 1), :]))

            dve.wait_ge(isum_done, 9)
            nc.vector.memset(iscore1[0:HALF, T - CHUNK:T], NOT_ADMITTED).then_inc(top_step, 1)
            nc.vector.memset(iscore0[0:HALF, P - CHUNK:P], NOT_ADMITTED).then_inc(top_step, 1)
            with dve.Fori(0, 4) as i:
                g = i + G_V

                def top_round(r):
                    pairs = ((iscore1, top1), (iscore0, top0))
                    dve.wait_ge(top_step, 8 * i + (4 * r + 2))
                    nc.vector.memset(carrier[:, :], 0.0)
                    for score, top in pairs:
                        nc.vector.max(top[:, :], score[:, :]).then_inc(top_step, 1)
                    dve.wait_ge(top_step, 8 * i + (4 * r + 4))
                    nc.vector.memset(carrier[:, :], 0.0)
                    for score, top in pairs:
                        nc.vector.match_replace(score[:, :], top[:, :], score[:, :], TAKEN).then_inc(top_step, 1)

                split_lo(g, 6)
                split_lo(g, 7)
                top_round(0)
                split_lo(g, 8)
                split_lo(g, 9)
                top_round(1)
                split_lo(g, 10)
                split_lo(g, 11)
                block_out(g, v_flat[:, ds(i * (TM * CB) + CB, CB)])
                split_lo(g, 12)
                split_lo(g, 13)

            dve.wait_ge(top_step, 34)
            nc.vector.tensor_scalar(dist1[:, :], iscore1[:, :], TAKEN, BIG, ALU.not_equal, ALU.mult).then_inc(pen_step, 1)
            nc.vector.tensor_scalar(dist0[:, :], iscore0[:, :], TAKEN, BIG, ALU.not_equal, ALU.mult).then_inc(pen_step, 1)
            dve.wait_ge(pen_step, 3)
            nc.vector.tensor_tensor(dist1[:, :], dist1[:, :], dist[:, :], ALU.add).then_inc(pen_step, 1)
            nc.vector.tensor_tensor(dist0[:, :], dist0[:, :], dist[:, P:T], ALU.add).then_inc(pen_step, 1)
            dve.wait_ge(bias_landed, 16)
            nc.vector.memset(bias[0:HALF, :, T - CHUNK:T], MASKED).then_inc(bias_masked, 1)
            dve.wait_ge(bias_masked, 1)
            dve.wait_ge(pen_step, 5)
            dve.wait_ge(cleared, 3 + HEADS)

            def maxima(pair):
                for t, p in enumerate((p1, p0)):
                    if t == 0:
                        dve.wait_ge(aux_read[0], pair + (AUX01_PAIRS + 1))
                    else:
                        dve.wait_ge(biased, pair + 1)
                    nc.vector.tensor_reduce(neg_max[:, t, :], p[:, :, :], AX.X, ALU.max,
                                            negate=True).then_inc(max_done, 1)

            def bias_b(pair):
                dve.wait_ge(scored, pair + 1)
                for t, (p, d, bank, n) in enumerate(((p1, dist1, aux[0], T), (p0, dist0, aux[1], P))):
                    for h in range(2):
                        last = nc.vector.scalar_tensor_tensor(p[:, h, :], d[:, :], neg_slope[:, ds(2 * pair + h, 1)],
                                                              bank[:, h * n:h * n + n], ALU.mult, ALU.add)
                    last.then_inc(aux_read[0] if t == 0 else biased, 1)

            def bias_a(i):
                pair = i + 4
                dve.wait_ge(scored, pair + 1)
                nc.vector.tensor_tensor(p1[:, :, :], aux[0][:, :].rearrange("p (h k) -> p h k", h=2),
                                        bias[:, ds(2 * i, 2), :], ALU.add).then_inc(aux_read[0], 1)
                nc.vector.tensor_tensor(p0[:, :, :], aux[1][:, 0:2 * P].rearrange("p (h k) -> p h k", h=2),
                                        bias[:, ds(2 * i, 2), P:T], ALU.add).then_inc(biased, 1)

            def pT1_out(pair):
                dve.wait_ge(exp_done, pair + 1)
                nc.vector.reciprocal(flat(p_inv[:, :, :]), flat(p_sum[:, :, :])).then_inc(inv_done, 1)
                dve.wait_ge(pt_done, pair + 1)
                nc.vector.tensor_copy(pT1[:, :, :, :].rearrange("p h k q -> p (h k q)"),
                                      aux[2][:, :]).then_inc(aux_read[2], 1)

            def outputs(pair):
                dve.wait_ge(pv_done, pair + 1)
                dve.wait_ge(inv_done, pair + 1)
                for t in range(2):
                    last = nc.vector.tensor_tensor(
                        o_flat[:, ds(place(pair, 1 - t), PAIR)].rearrange("p (h d) -> p h d", h=2),
                        aux[3][:, t * PAIR:t * PAIR + PAIR].rearrange("p (h d) -> p h d", h=2),
                        p_inv[:, t, :].unsqueeze(2).broadcast_to((P, 2, HD)), ALU.mult)
                last.then_inc(aux_read[3], 1)

            with dve.Fori(0, 4) as i:
                g = i + G_QKA
                split_lo(g, 6)
                bias_b(i)
                maxima(i)
                split_lo(g, 7)
                split_lo(g, 8)
                pT1_out(i)
                split_lo(g, 9)
                split_lo(g, 10)
                outputs(i)
                split_lo(g, 11)
                block_out(g, stage[:, 1, :], 2 * i + 2 * G_V)
                split_lo(g, 12)
                split_lo(g, 13)
                second_half_out(i + G_V, flat(qk[:, ds(2 * i + 1, 1), :]))

            def gate_block(g, i):
                split_lo(g, 6)
                bias_a(i)
                maxima(i + 4)
                split_lo(g, 7)
                split_lo(g, 8)
                pT1_out(i + 4)
                split_lo(g, 9)
                split_lo(g, 10)
                outputs(i + 4)

            def gated(g, i, m):
                ob = o_flat[:, ds(i * (TM * CB) + m * CB, CB)]
                dve.wait_ge(tanh_done, 2 * i + (m + 1))
                dve.wait_ge(aux_read[3], i + (AUX23_A + 1))
                nc.vector.scalar_tensor_tensor(ob, acc[:, ds((g % 2) * (TM * CB) + m * CB, CB)],
                                               half_rstd[:, m:m + 1], ob, ALU.mult, ALU.mult).then_inc(acc_out[m], 1)
                dve.wait_ge(acc_out[m], g + 1)
                nc.vector.scalar_tensor_tensor(ob, t_gate[:, m, :], 1.0, ob, ALU.add, ALU.mult).then_inc(y_done, 1)

            with dve.Fori(0, 3) as i:
                g = i + G_GATE
                gate_block(g, i)
                split_lo(g, 11)
                for m in range(TM):
                    gated(g, i, m)
                split_lo(g, 12)
                split_lo(g, 13)

            def y_lo(q):
                dve.wait_ge(yhi_done, q + 1)
                nc.vector.tensor_tensor(flat(a_lo[:, UK * q:UK * q + UK, :]), aux[q % 4][:, :],
                                        flat(a_hi[:, UK * q:UK * q + UK, :]).bitcast(f32),
                                        ALU.subtract).then_inc(ylo_done, 1)

            gate_block(G_OUT - 1, 3)
            y_lo(0)
            gated(G_OUT - 1, 3, 0)
            y_lo(1)
            gated(G_OUT - 1, 3, 1)
            split_lo(G_OUT, 3)
            y_lo(2)
            y_lo(3)
            for q in range(4, 8):
                y_lo(q)
                split_lo(G_OUT, q)

            def residual(g, b, tiles=(0, 1)):
                for m in tiles:
                    nc.vector.tensor_tensor(z[:, m, :], acc[:, ds((g % 2) * (TM * CB) + m * CB, CB)],
                                            v_flat[:, ds(m * D + b * CB, CB)], ALU.add).then_inc(acc_out[m], 1)
                for m in tiles:
                    dve.wait_ge(acc_out[m], g + 1)
                    nc.vector.tensor_tensor(o_flat[:, ds(m * D + b * CB, CB)], z[:, m, :], fgain[:, ds(b * CB, CB)],
                                            ALU.mult).then_inc(zg_done, 1)

            for c in range(8, 12):
                split_lo(G_OUT, c)
            dve.wait_ge(res_landed, 16)
            dve.wait_ge(fgain_landed, 16)
            dve.wait_ge(mm_done, G_OUT * UNITS + UNITS)
            residual(G_OUT, 0)
            with dve.Fori(1, 3) as b:
                for c in range(4, 12):
                    split_lo(b + G_OUT, c)
                dve.wait_ge(zsq_done, 2 * b)
                dve.wait_ge(mm_done, b * UNITS + (G_OUT * UNITS + UNITS))
                residual(b + G_OUT, b)
            for c in range(4, 8):
                split_lo(G_END - 1, c)
            dve.wait_ge(zsq_done, 6)
            for m in range(TM):
                dve.wait_ge(tail_done, m + 1)
                residual(G_END - 1, 3, (m,))
                dve.wait_ge(zsq_done, 7 + m)
                nc.vector.tensor_reduce(zrstd[:, m:m + 1], zsq[:, m, :], AX.X, ALU.add).then_inc(fin_sum, 1)
                dve.wait_ge(fin_sum, m + 1)
                nc.vector.tensor_scalar(zrstd[:, m:m + 1], zrstd[:, m:m + 1], 1.0 / D, EPS, ALU.mult,
                                        ALU.add).then_inc(var_done, 1)
                dve.wait_ge(fin_std, m + 1)
                nc.vector.reciprocal(zrstd[:, m:m + 1], zrstd[:, m:m + 1]).then_inc(fin_rstd, 1)
                dve.wait_ge(fin_rstd, m + 1)
                dve.wait_ge(zg_done, 7 + m)
                for h in (h for tile, h in VECTOR_QUARTERS if tile == m):
                    c = slice(h * (D // 2), (h + 1) * (D // 2))
                    nc.vector.tensor_scalar(z_gain[:, m, c], z_gain[:, m, c], zrstd[:, m:m + 1], None,
                                            ALU.mult).then_inc(fin_ready[1], 1)


_OFFSETS = {"qa": 0, "ka": 1024, "va": 2048, "ga": 3072, "qb": 4096, "kb": 5120, "vb": 6144, "gb": 7168, "qi": 8192}
_STREAM = ["qi", "qb", "kb", "vb", "va", "qa", "ka", "gb", "ga"]


def kernel(x, norm_gain, w_in, rel_bias, w_out, final_gain):
    import numpy as np
    import concourse.bacc as bacc
    from concourse.bass_utils import run_bass_kernel_spmd

    x, w_in, w_out = np.asarray(x)[0], np.asarray(w_in)[0], np.asarray(w_out)[0]

    def units(w):
        return w.reshape(UNITS, UK, P, CB).transpose(0, 2, 1, 3).reshape(UNITS, P, UK * CB)

    starts = [_OFFSETS[name] + half * CB for name in _STREAM for half in range(2)]
    narrow = w_in[:, 9216:9216 + NARROW]
    w_out = np.concatenate([w_out[D // 2:], w_out[:D // 2]])
    arrays = {
        "xT": x.T.reshape(KT, P, T).transpose(1, 0, 2),
        "x": x.reshape(TM, P, D).transpose(1, 0, 2),
        "norm_gain": np.asarray(norm_gain)[0].reshape(KT, P).T,
        "w_blocks": np.stack([units(w_in[:, c:c + CB]) for c in starts]),
        "w_narrow": narrow.reshape(KT, P, NARROW).transpose(1, 0, 2).reshape(P, KT * NARROW),
        "rel_bias": np.asarray(rel_bias)[0],
        "wo_blocks": np.stack([units(w_out[:, c:c + CB]) for c in range(0, D, CB)]),
        "final_gain": np.asarray(final_gain),
    }
    arrays = {name: np.ascontiguousarray(a) for name, a in arrays.items()}
    nc = bacc.Bacc("TRN2", target_bir_lowering=False, num_devices=1)
    args = [nc.dram_tensor(name, a.shape, mybir.dt.from_np(a.dtype), kind="ExternalInput").ap()
            for name, a in arrays.items()]
    out = nc.dram_tensor("out", (T, D), mybir.dt.float32, kind="ExternalOutput").ap()
    hybrid_block(nc, *args, out)
    r = run_bass_kernel_spmd(nc, [arrays], core_ids=[0])
    return r.results[0]["out"].reshape(1, T, D)
```

```python
import concourse.bass as bass
from concourse import mybir
from contextlib import ExitStack

P = 128
D = 2048
T = 256
TM = T // P
KT = D // P
CB = 512
HD = 128
HEADS = 8
CHUNK = 64
MAX_REL = 128
IDX_H, IDX_D = 16, 64
TOP = 64
EPS = 1e-6
NARROW = IDX_D + IDX_H
QK_SCALE = HD ** -0.5
IDX_SCALE = IDX_H ** -0.5 * IDX_D ** -0.5
BIG = 1e30
MASKED = -1e30
NOT_ADMITTED = -1e38
TAKEN = -3e38

G_QB, G_V, G_QKA, G_GATE, G_OUT, G_END = 2, 6, 10, 14, 18, 22
UK = 2
UNITS = KT // UK
RING = 4
HALVED = 2


def hybrid_block(nc, xT, x, norm_gain, w_blocks, w_narrow, rel_bias, wo_blocks, final_gain, out):
    f32 = mybir.dt.float32
    f32r = mybir.dt.float32r
    ALU = mybir.AluOpType
    ACT = mybir.ActivationFunctionType
    AX = mybir.AxisListType
    ds = bass.ds

    with ExitStack() as ctx:
        def sb(name, shape, dt=f32):
            return ctx.enter_context(nc.sbuf_tensor(name, shape, dt))

        def pb(name, shape):
            return ctx.enter_context(nc.psum_tensor(name, shape, f32))

        def sem(name):
            return ctx.enter_context(nc.semaphore(name))

        w_raw = sb("w_raw", [P, RING, UK * CB])
        w_hi = sb("w_hi", [P, RING, UK, CB], f32r)
        w_lo = sb("w_lo", [P, RING, UK, CB], f32r)
        nw_raw = sb("nw_raw", [P, KT * NARROW])
        nw_hi = sb("nw_hi", [P, KT, NARROW], f32r)
        nw_lo = sb("nw_lo", [P, KT, NARROW], f32r)
        a_hi = sb("a_hi", [P, KT, T], f32r)
        a_lo = sb("a_lo", [P, KT, T], f32r)
        v = sb("v", [P, 4, TM, CB])
        x_nat = v[:, :, :, :].rearrange("p b m c -> p (b m c)").rearrange("p (m d) -> p m d", m=TM)
        o = sb("o", [P, 4, TM, CB])
        z_gain = o[:, :, :, :].rearrange("p b m c -> p (b m c)").rearrange("p (m d) -> p m d", m=TM)
        qk = sb("qk", [P, 8, 2 * T])
        qiT = sb("qiT", [P, 4, 2 * T])
        q_now = sb("q_now", [P, 2, T])
        stage = sb("stage", [P, TM, CB])
        ki_bd = sb("ki_bd", [P, 2, T])
        ki_nat = sb("ki_nat", [P, TM, P])
        narrow = sb("narrow", [NARROW, T])
        w_idx = sb("w_idx", [P, TM, IDX_H])
        relu1 = sb("relu1", [P, 2, T])
        relu0 = sb("relu0", [P, 2, P])
        iscore1 = sb("iscore1", [P, T])
        iscore0 = sb("iscore0", [P, P])
        top1 = sb("top1", [P, 8])
        top0 = sb("top0", [P, 8])
        carrier = sb("carrier", [P, 1])
        dist = sb("dist", [P, T])
        dist1 = sb("dist1", [P, T])
        dist0 = sb("dist0", [P, P])
        bias = sb("bias", [P, HEADS, T])
        bias_ext = sb("bias_ext", [HEADS, 3 * P])
        bias_row = sb("bias_row", [HEADS, 2 * MAX_REL + 1])
        neg_slope = sb("neg_slope", [P, HEADS])
        qscale = sb("qscale", [P, 1])
        ones = sb("ones", [P, 1])
        p1 = sb("p1", [P, 2, T])
        p0 = sb("p0", [P, 2, P])
        pT1 = sb("pT1", [P, 2, 2, P])
        pT0 = sb("pT0", [P, 2, P])
        neg_max = sb("neg_max", [P, 2, 2])
        p_sum = sb("p_sum", [P, 2, 2])
        p_inv = sb("p_inv", [P, 2, 2])
        t_gate = sb("t_gate", [P, TM, CB])
        z = sb("z", [P, TM, CB])
        ident = sb("ident", [P, P])
        gain = sb("gain", [P, KT])
        fgain = sb("fgain", [P, D])
        ssq = sb("ssq", [P, TM])
        rstd = sb("rstd", [P, TM])
        half_rstd = sb("half_rstd", [P, TM])
        zsq = sb("zsq", [P, TM, 4])
        zpart = sb("zpart", [P, TM])
        zrstd = sb("zrstd", [P, TM])

        xT_land = qk[:, :, :].rearrange("p c t -> p (c t)").rearrange("p (k t) -> p k t", k=KT)

        acc = pb("acc", [P, 4 * CB])
        aux = [pb(f"aux{i}", [P, CB]) for i in range(4)]

        w_landed = [sem(f"w_landed{s}") for s in range(RING)]
        hi_done = sem("hi_done")
        lo_done = sem("lo_done")
        mm_done = sem("mm_done")
        xT0_landed = sem("xT0_landed")
        half_landed = [sem(f"half_landed{u}") for u in range(HALVED)]
        xT_landed = [sem(f"xT_landed{c}") for c in range(UNITS)]
        nw_landed = sem("nw_landed")
        gain_landed = sem("gain_landed")
        row_landed = sem("row_landed")
        fgain_landed = sem("fgain_landed")
        ext_ready = sem("ext_ready")
        ext_stored = sem("ext_stored")
        bias_landed = sem("bias_landed")
        res_landed = sem("res_landed")
        out_landed = sem("out_landed")
        cleared = sem("cleared")
        patterned = sem("patterned")
        ahi_done = sem("ahi_done")
        alo_done = sem("alo_done")
        half_hi = sem("half_hi")
        half_lo = sem("half_lo")
        nhi_done = sem("nhi_done")
        nlo_done = sem("nlo_done")
        sq_step = sem("sq_step")
        ssq_done = sem("ssq_done")
        var_done = sem("var_done")
        std_done = sem("std_done")
        rstd_done = sem("rstd_done")
        narrow_done = sem("narrow_done")
        kit_done = sem("kit_done")
        aux_read = [sem(f"aux{i}_read") for i in range(4)]
        acc_out = [sem("acc0_out"), sem("acc1_out")]
        tr_done = sem("tr_done")
        khi_done = sem("khi_done")
        klo_done = sem("klo_done")
        qhi_done = sem("qhi_done")
        qnow_ready = sem("qnow_ready")
        iscored = sem("iscored")
        isum_done = sem("isum_done")
        isum_step = sem("isum_step")
        top_step = sem("top_step")
        pen_step = sem("pen_step")
        bias_masked = sem("bias_masked")
        scored = sem("scored")
        biased = sem("biased")
        max_done = sem("max_done")
        exp_done = sem("exp_done")
        inv_done = sem("inv_done")
        pt_done = sem("pt_done")
        pv_done = sem("pv_done")
        tanh_done = sem("tanh_done")
        y_done = sem("y_done")
        ytr_done = sem("ytr_done")
        yhi_done = sem("yhi_done")
        ylo_done = sem("ylo_done")
        zsq_done = sem("zsq_done")
        zg_done = sem("zg_done")
        tail_done = sem("tail_done")
        part_sum = sem("part_sum")
        part_var = sem("part_var")
        fin_std = sem("fin_std")
        fin_rstd = sem("fin_rstd")
        scalar_scaled = sem("scalar_scaled")
        vector_scaled = sem("vector_scaled")

        bias_dram = nc.dram_tensor("bias_dram", (P, HEADS, T), f32, kind="Internal").ap()

        AUX01_INDEX, AUX01_PAIRS, AUX01_Y = 2, 10, 18
        AUX23_BLOCKS, AUX23_B, AUX23_A, AUX23_Y = 0, 6, 14, 18
        HALF = CHUNK

        def flat(t):
            return t.rearrange("p a b -> p (a b)")

        v_flat = v[:, :, :, :].rearrange("p b m c -> p (b m c)")
        o_flat = o[:, :, :, :].rearrange("p b m c -> p (b m c)")
        qnow_flat = flat(q_now[:, :, :])
        nhi_flat, nlo_flat = flat(nw_hi[:, :, :]), flat(nw_lo[:, :, :])
        ki_hi, ki_lo = nhi_flat[:, 0:2 * T], nlo_flat[:, 0:2 * T]
        qi_hi, qi_lo = nhi_flat[:, 2 * T:4 * T], nlo_flat[:, 2 * T:4 * T]
        sq_sum, sq_x = o_flat[:, 0:UK * T], o_flat[:, UK * T:2 * UK * T]
        PAIR = 2 * HD
        VECTOR_PARTS = ((0, slice(0, D // 2)), (0, slice(D // 2, D)), (1, slice(0, CB)), (1, slice(2 * CB, D)))
        SCALAR_PART = slice(CB, 2 * CB)

        def place(pair, m):
            return (pair // 2) * (TM * CB) + (pair % 2) * PAIR + m * CB

        block = ctx.enter_context(nc.Block())

        @block.sync
        def _(sp):
            def load(u, src):
                sp.dma_start(w_raw[:, u % RING, :], src).then_inc(w_landed[u % RING], 16)

            sp.dma_start(gain[:, :], norm_gain).then_inc(gain_landed, 16)
            sp.dma_start(xT_land[:, 0, :], xT[:, 0, :]).then_inc(xT0_landed, 16)
            for u in range(HALVED):
                sp.dma_start(w_raw[:, u, 0:CB], w_blocks[0, u, :, 0:CB]).then_inc(half_landed[u], 16)
                if u == 0:
                    sp.dma_start(xT_land[:, 1, :], xT[:, 1, :]).then_inc(xT_landed[0], 16)
                sp.dma_start(w_raw[:, u, CB:2 * CB], w_blocks[0, u, :, CB:2 * CB]).then_inc(w_landed[u], 16)
                k = slice(UK * (u + 1), UK * (u + 2))
                sp.dma_start(xT_land[:, k, :], xT[:, k, :]).then_inc(xT_landed[u + 1], 16)
            for u in range(HALVED, UNITS):
                if u > HALVED:
                    k = slice(UK * u, UK * u + UK)
                    sp.dma_start(xT_land[:, k, :], xT[:, k, :]).then_inc(xT_landed[u], 16)
                if u >= RING:
                    sp.wait_ge(lo_done, u - RING + 1)
                load(u, w_blocks[0, u, :, :])
            sp.dma_start(nw_raw[:, :], w_narrow).then_inc(nw_landed, 16)
            with sp.Fori(1, G_OUT) as g:
                for u in range(UNITS):
                    sp.wait_ge(lo_done, g * UNITS + (u - RING + 1))
                    load(u, w_blocks[ds(g, 1), u, :, :].rearrange("o p c -> (o p) c"))
            with sp.Fori(G_OUT, G_END) as g:
                for u in range(UNITS):
                    sp.wait_ge(lo_done, g * UNITS + (u - RING + 1))
                    load(u, wo_blocks[ds(g - G_OUT, 1), u, :, :].rearrange("o p c -> (o p) c"))
            for n, (m, c) in enumerate(VECTOR_PARTS):
                sp.wait_ge(vector_scaled, n + 1)
                sp.dma_start(out[m * P:m * P + P, c], z_gain[:, m, c]).then_inc(out_landed, 16)
            sp.wait_ge(out_landed, 16 * (len(VECTOR_PARTS) + 1))

        @block.gpsimd
        def _(pool):
            pool.dma_start(bias_row[:, :], rel_bias).then_inc(row_landed, 16)
            nc.gpsimd.memset(ki_bd[:, :, :], 0.0).then_inc(cleared, 1)
            nc.gpsimd.memset(ident[:, :], 0.0).then_inc(cleared, 1)
            nc.gpsimd.memset(ones[:, :], 1.0).then_inc(cleared, 1)
            nc.gpsimd.memset(qscale[:, :], QK_SCALE).then_inc(cleared, 1)
            for h in range(HEADS):
                nc.gpsimd.memset(neg_slope[:, h:h + 1], -(2.0 ** (-8.0 * (h + 1) / HEADS))).then_inc(cleared, 1)
            pool.wait_ge(cleared, 4 + HEADS)
            nc.gpsimd.affine_select(out=ident[:, :], in_=ident[:, :], compare_op=ALU.not_equal, fill=1.0,
                                    base=0, pattern=[[-1, P]], channel_multiplier=1).then_inc(patterned, 1)
            nc.gpsimd.iota(dist[:, :], pattern=[[-1, T]], base=P, channel_multiplier=1,
                           allow_small_or_imprecise_dtypes=True).then_inc(patterned, 1)
            pool.wait_ge(xT0_landed, 16)
            for u in range(UNITS):
                pool.wait_ge(xT_landed[u], 16)
                x_u = flat(xT_land[:, UK * u:UK * u + UK, :])
                if u == 0:
                    nc.gpsimd.tensor_tensor(sq_sum, x_u, x_u, ALU.mult).then_inc(sq_step, 1)
                    continue
                pool.wait_ge(sq_step, 2 * u - 1)
                nc.gpsimd.tensor_tensor(sq_x, x_u, x_u, ALU.mult).then_inc(sq_step, 1)
                pool.wait_ge(sq_step, 2 * u)
                nc.gpsimd.tensor_tensor(sq_sum, sq_sum, sq_x, ALU.add).then_inc(sq_step, 1)

            def split_q(i):
                pool.wait_ge(aux_read[2], AUX23_BLOCKS + 1 + i // 2)
                pool.wait_ge(aux_read[3], AUX23_BLOCKS + 1 + i // 2)
                chunk = qiT[:, i, :]
                nc.gpsimd.tensor_tensor(qi_hi, chunk, ones[:, :].broadcast_to((P, 2 * T)),
                                        ALU.mult).then_inc(qhi_done, 1)
                pool.wait_ge(qhi_done, i + 1)
                nc.gpsimd.tensor_tensor(qi_lo, chunk, qi_hi.bitcast(f32), ALU.subtract).then_inc(qnow_ready, 1)

            pool.wait_ge(narrow_done, 1)
            split_q(0)
            for i in range(1, 4):
                pool.wait_ge(iscored, 2 * i)
                split_q(i)

            pool.wait_ge(ext_ready, 2)
            ext = bias_ext[:, :]
            windows = bass.AP(tensor=ext.tensor, offset=ext.offset + P - 1, ap=[list(ext.ap[0]), [-1, P], [1, T]])
            pool.dma_start(bias_dram.rearrange("p h c -> h p c"), windows).then_inc(ext_stored, 16)
            pool.wait_ge(ext_stored, 16)
            pool.dma_start(bias[:, :, :], bias_dram).then_inc(bias_landed, 16)
            pool.dma_start(fgain[:, :], final_gain.partition_broadcast(P)).then_inc(fgain_landed, 16)

            def scaled(chunk):
                nc.gpsimd.tensor_tensor(qnow_flat, flat(qk[:, ds(chunk, 1), :]),
                                        qscale[:, :].broadcast_to((P, 2 * T)), ALU.mult).then_inc(qnow_ready, 1)

            pool.wait_ge(iscored, 2 * 4)
            pool.wait_ge(aux_read[2], AUX23_B)
            pool.wait_ge(aux_read[3], AUX23_B)
            scaled(0)
            with pool.Fori(1, 4) as i:
                pool.wait_ge(scored, i)
                scaled(2 * i)
            with pool.Fori(0, 4) as i:
                pool.wait_ge(scored, i + 4)
                pool.wait_ge(aux_read[2], (i // 2) * 2 + (AUX23_B + 2))
                pool.wait_ge(aux_read[3], (i // 2) * 2 + (AUX23_B + 2))
                scaled(i)
            pool.wait_ge(pv_done, HEADS)
            pool.dma_start(x_nat, x).then_inc(res_landed, 16)

        @block.tensor
        def _(pe):
            def mm3(dst, k, m, hi, lo, start, stop):
                t = slice(m * P, m * P + P)
                nc.tensor.matmul(dst, a_hi[:, k, t], hi, start=start, stop=False)
                nc.tensor.matmul(dst, a_hi[:, k, t], lo, start=False, stop=False)
                return nc.tensor.matmul(dst, a_lo[:, k, t], hi, start=False, stop=stop)

            def unit(g, u):
                if u == 0 and not (isinstance(g, int) and g < 2):
                    pe.wait_ge(acc_out[0], g - 1)
                    pe.wait_ge(acc_out[1], g - 1)
                pe.wait_ge(lo_done, g * UNITS + (u + 1))
                for kk in range(UK):
                    k = u * UK + kk
                    for m in range(TM):
                        dst = acc[:, ds((g % 2) * (TM * CB) + m * CB, CB)]
                        last = mm3(dst, k, m, w_hi[:, u % RING, kk, :], w_lo[:, u % RING, kk, :],
                                   k == 0, k == KT - 1)
                last.then_inc(mm_done, 1)

            def transposes(tb, g, used):
                pe.wait_ge(acc_out[0], g + 1)
                pe.wait_ge(acc_out[1], g + 1)
                for half in range(2):
                    if used is not None:
                        pe.wait_ge(aux_read[2 + half], used)
                    for h in range(2):
                        for m in range(TM):
                            c = (2 * half + h) * HD
                            last = nc.tensor.transpose(aux[2 + half][:, h * T + m * P:h * T + m * P + P],
                                                       stage[:, m, c:c + HD], ident[:, :])
                    last.then_inc(tr_done, 1)

            pe.wait_ge(cleared, 1)
            for m in range(TM):
                nc.tensor.matmul(acc[:, m * CB:m * CB + CB], ki_bd[:, 0, 0:P], ki_bd[:, :, :],
                                 start=True, stop=True)
            for u in range(HALVED):
                for kk in range(UK):
                    k = u * UK + kk
                    pe.wait_ge(alo_done, k + 1)
                    pe.wait_ge((half_lo, lo_done)[kk], u + 1)
                    for m in range(TM):
                        last = mm3(acc[:, m * CB:m * CB + CB], k, m, w_hi[:, u, kk, :], w_lo[:, u, kk, :],
                                   k == 0, False)
                last.then_inc(mm_done, 1)
            for u in range(HALVED, UNITS):
                pe.wait_ge(alo_done, UK * u + UK)
                unit(0, u)
            unit(1, 0)
            pe.wait_ge(sq_step, 2 * UNITS - 1)
            for m in range(TM):
                for k in range(UK):
                    last = nc.tensor.matmul(aux[1][:, m:m + 1], sq_sum[:, k * T + m * P:k * T + m * P + P],
                                            ones[:, :], start=(k == 0), stop=(k == UK - 1))
            last.then_inc(ssq_done, 1)
            for u in range(1, 4):
                unit(1, u)
            pe.wait_ge(patterned, 1)
            transposes(0, 0, None)
            unit(1, 4)
            unit(1, 5)

            pe.wait_ge(nlo_done, 1)
            for k in range(KT):
                for n, (w, a) in enumerate(((nw_hi, a_hi), (nw_hi, a_lo), (nw_lo, a_hi))):
                    last = nc.tensor.matmul(aux[0][0:NARROW, 0:T], w[:, k, :], a[:, k, :],
                                            start=(k == 0 and n == 0), stop=(k == KT - 1 and n == 2))
            last.then_inc(narrow_done, 1)
            unit(1, 6)
            pe.wait_ge(aux_read[0], 1)
            pe.wait_ge(var_done, 1)
            for m in range(TM):
                last = nc.tensor.transpose(aux[1][:, m * P:m * P + NARROW], narrow[:, m * P:m * P + P],
                                           ident[0:NARROW, 0:NARROW])
            last.then_inc(narrow_done, 1)
            unit(1, 7)
            pe.wait_ge(aux_read[1], 2)
            for m in range(TM):
                last = nc.tensor.transpose(aux[0][:, m * P:m * P + P], ki_nat[:, m, :], ident[:, :])
            last.then_inc(kit_done, 1)
            unit(2, 0)
            unit(2, 1)
            transposes(1, 1, 1)

            with pe.Fori(0, 4) as i:
                g = i + G_QB

                def index_pair(c):
                    pe.wait_ge(klo_done, 1)
                    pe.wait_ge(qnow_ready, i + 1)
                    pe.wait_ge(aux_read[0], 2 * i + (AUX01_INDEX + c))
                    pe.wait_ge(aux_read[1], 2 * i + (AUX01_INDEX + c))
                    for n, (q, k) in enumerate(((qi_hi, ki_hi), (qi_hi, ki_lo), (qi_lo, ki_hi))):
                        nc.tensor.matmul(aux[0][:, :], q[:, c * T + P:c * T + T], k, start=(n == 0), stop=(n == 2))
                    for n, (q, k) in enumerate(((qi_hi, ki_hi), (qi_hi, ki_lo), (qi_lo, ki_hi))):
                        last = nc.tensor.matmul(aux[1][:, 0:2 * P], q[:, c * T:c * T + P],
                                                k.rearrange("p (h t) -> p h t", h=2)[:, :, 0:P],
                                                start=(n == 0), stop=(n == 2))
                    last.then_inc(iscored, 1)

                unit(g, 2)
                index_pair(0)
                unit(g, 3)
                unit(g, 4)
                index_pair(1)
                for u in range(5, UNITS):
                    unit(g, u)
                unit(g + 1, 0)
                unit(g + 1, 1)
                transposes(g, g, i + (AUX23_BLOCKS + G_QB))

            with pe.Fori(G_V, G_QKA) as g:
                for u in range(2, UNITS):
                    unit(g, u)
                unit(g + 1, 0)
                unit(g + 1, 1)

            def score_pair(pair, k_chunk):
                pe.wait_ge(qnow_ready, pair + 5)
                pe.wait_ge(aux_read[0], pair + AUX01_PAIRS)
                pe.wait_ge(aux_read[1], pair + AUX01_PAIRS)
                for h in range(2):
                    nc.tensor.matmul(aux[0][:, h * T:h * T + T], q_now[:, h, P:T],
                                     flat(qk[:, ds(k_chunk, 1), h * T:h * T + T]), start=True, stop=True)
                for h in range(2):
                    last = nc.tensor.matmul(aux[1][:, h * P:h * P + P], q_now[:, h, 0:P],
                                            flat(qk[:, ds(k_chunk, 1), h * T:h * T + P]), start=True, stop=True)
                last.then_inc(scored, 1)

            def transpose_pair(pair, used2):
                pe.wait_ge(exp_done, pair + 1)
                pe.wait_ge(aux_read[2], used2)
                for h in range(2):
                    for kt in range(TM):
                        c = (2 * h + kt) * P
                        nc.tensor.transpose(aux[2][:, c:c + P], p1[:, h, kt * P:kt * P + P], ident[:, :])
                for h in range(2):
                    last = nc.tensor.transpose(aux[1][:, h * P:h * P + P], p0[:, h, :], ident[:, :])
                last.then_inc(pt_done, 1)

            def value_pair(pair, used2, used3):
                pe.wait_ge(aux_read[2], used2 + 1)
                pe.wait_ge(aux_read[1], pair + (AUX01_PAIRS + 1))
                pe.wait_ge(aux_read[3], used3)
                for h in range(2):
                    for kt in range(TM):
                        nc.tensor.matmul(aux[3][:, h * HD:h * HD + HD], pT1[:, h, kt, :],
                                         v_flat[:, ds(place(pair, kt) + h * HD, HD)],
                                         start=(kt == 0), stop=(kt == TM - 1))
                for h in range(2):
                    last = nc.tensor.matmul(aux[3][:, (2 + h) * HD:(3 + h) * HD], pT0[:, h, :],
                                            v_flat[:, ds(place(pair, 0) + h * HD, HD)], start=True, stop=True)
                last.then_inc(pv_done, 1)

            with pe.Fori(0, 4) as i:
                g = i + G_QKA
                used = 2 * i + AUX23_B
                unit(g, 2)
                score_pair(i, 2 * i + 1)
                for u in (3, 4, 5):
                    unit(g, u)
                transpose_pair(i, used)
                unit(g, 6)
                value_pair(i, used, used)
                unit(g, 7)
                unit(g + 1, 0)
                unit(g + 1, 1)
                transposes(None, g, used + 1)

            def gate_block(g, i):
                used = i + AUX23_A
                unit(g, 2)
                pe.wait_ge(aux_read[2], (i // 2) * 2 + (AUX23_B + 6))
                pe.wait_ge(aux_read[3], (i // 2) * 2 + (AUX23_B + 6))
                score_pair(i + 4, i + 4)
                for u in (3, 4, 5):
                    unit(g, u)
                transpose_pair(i + 4, used)
                unit(g, 6)
                value_pair(i + 4, used, used)
                unit(g, 7)

            with pe.Fori(0, 3) as i:
                gate_block(i + G_GATE, i)
                unit(i + (G_GATE + 1), 0)
                unit(i + (G_GATE + 1), 1)
            gate_block(G_OUT - 1, 3)

            def y_transposes(q):
                pe.wait_ge(y_done, 2 * (q // 2) + 2)
                if q < 4:
                    pe.wait_ge(aux_read[q], AUX01_Y if q < 2 else AUX23_Y)
                else:
                    pe.wait_ge(ylo_done, q - 3)
                for kk in range(UK):
                    for m in range(TM):
                        c = (q % 2) * PAIR + kk * HD
                        last = nc.tensor.transpose(aux[q % 4][:, kk * T + m * P:kk * T + m * P + P],
                                                   o[:, q // 2, m, c:c + HD], ident[:, :])
                last.then_inc(ytr_done, 1)

            for q in range(4):
                y_transposes(q)
            for u in range(UNITS):
                pe.wait_ge(ylo_done, u + 1)
                unit(G_OUT, u)
                if u < 4:
                    y_transposes(u + 4)
            with pe.Fori(G_OUT + 1, G_END - 1) as g:
                for u in range(UNITS):
                    unit(g, u)
            g = G_END - 1
            for u in range(UNITS - RING):
                unit(g, u)
            for m in range(TM):
                for u in range(UNITS - RING, UNITS):
                    pe.wait_ge(lo_done, g * UNITS + (u + 1))
                    for kk in range(UK):
                        k = u * UK + kk
                        bank = ((g % 2) * TM + m) * CB
                        last = mm3(acc[:, bank:bank + CB], k, m, w_hi[:, u % RING, kk, :], w_lo[:, u % RING, kk, :],
                                   False, k == KT - 1)
                last.then_inc(tail_done, 1)

        @block.scalar
        def _(act):
            def split_hi(g, c):
                u = c % UNITS
                s = u % RING
                act.wait_ge(w_landed[s], g * (16 * UNITS // RING) + 16 * (c // RING + 1))
                if not (isinstance(g, int) and g * UNITS + c < RING):
                    act.wait_ge(mm_done, g * UNITS + (c - RING + 1))
                nc.scalar.activation(flat(w_hi[:, s, :, :]), w_raw[:, s, :], ACT.Copy).then_inc(hi_done, 1)

            def block_out(g, dst, tr=None):
                act.wait_ge(mm_done, g * UNITS + UNITS)
                if tr is not None:
                    act.wait_ge(tr_done, tr)
                nc.scalar.activation(dst, acc[:, ds((g % 2) * (TM * CB), CB)], ACT.Copy,
                                     scale=rstd[:, 0:1]).then_inc(acc_out[0], 1)

            def first_half_out(tb, dst):
                act.wait_ge(tr_done, 2 * tb + 1)
                nc.scalar.activation(dst, aux[2][:, :], ACT.Copy).then_inc(aux_read[2], 1)

            nc.scalar.preload_act_table(ACT.Exp)
            act.wait_ge(gain_landed, 16)

            def a_part(k):
                nc.scalar.activation(a_hi[:, k, :], xT_land[:, k, :], ACT.Copy,
                                     scale=gain[:, k:k + 1]).then_inc(ahi_done, 1)

            for u in range(HALVED):
                for kk in range(UK):
                    if u + kk == 0:
                        act.wait_ge(xT0_landed, 16)
                    elif u == 0 or kk == 0:
                        act.wait_ge(xT_landed[u], 16)
                    a_part(u * UK + kk)
                    act.wait_ge((half_landed, w_landed)[kk][u], 16)
                    nc.scalar.activation(w_hi[:, u, kk, :], w_raw[:, u, kk * CB:kk * CB + CB],
                                         ACT.Copy).then_inc((half_hi, hi_done)[kk], 1)
            for u in range(HALVED, UNITS):
                act.wait_ge(xT_landed[u], 16)
                for k in range(UK * u, UK * u + UK):
                    a_part(k)
                split_hi(0, u)
            nc.scalar.preload_act_table(ACT.Sqrt)
            for c in (8, 9, 10):
                split_hi(0, c)
            act.wait_ge(nw_landed, 16)
            nc.scalar.activation(flat(nw_hi[:, :, :]), nw_raw[:, :], ACT.Copy).then_inc(nhi_done, 1)
            act.wait_ge(var_done, 1)
            nc.scalar.activation(rstd[:, :], ssq[:, :], ACT.Sqrt).then_inc(std_done, 1)
            for c in (11, 12):
                split_hi(0, c)
            nc.scalar.preload_act_table(ACT.Exp)
            split_hi(0, 13)
            act.wait_ge(rstd_done, 2)
            block_out(0, stage[:, 0, :])
            split_hi(0, 14)
            split_hi(0, 15)
            first_half_out(0, qiT[:, 0, :])
            split_hi(0, 16)
            split_hi(0, 17)
            act.wait_ge(narrow_done, 1)
            nc.scalar.activation(narrow[:, :], aux[0][0:NARROW, 0:T], ACT.Copy).then_inc(aux_read[0], 1)
            split_hi(0, 18)
            act.wait_ge(aux_read[0], 2)
            nc.scalar.activation(ki_hi, flat(ki_bd[:, :, :]), ACT.Copy).then_inc(khi_done, 1)
            split_hi(0, 19)
            block_out(1, stage[:, 0, :], 2)
            split_hi(0, 20)
            split_hi(0, 21)
            first_half_out(1, qiT[:, 2, :])

            with act.Fori(0, 4) as i:
                g = i + G_QB

                def index_relu(c):
                    act.wait_ge(iscored, 2 * i + (c + 1))
                    act.wait_ge(isum_done, 2 * i + (c + 1))
                    nc.scalar.activation(flat(relu1[:, :, :]), aux[0][:, :], ACT.Relu).then_inc(aux_read[0], 1)
                    nc.scalar.activation(flat(relu0[:, :, :]), aux[1][:, 0:2 * P],
                                         ACT.Relu).then_inc(aux_read[1], 1)

                split_hi(g, 6)
                index_relu(0)
                split_hi(g, 7)
                split_hi(g, 8)
                index_relu(1)
                for c in (9, 10, 11):
                    split_hi(g, c)
                block_out(g, stage[:, 0, :], 2 * i + 2 * G_QB)
                split_hi(g, 12)
                split_hi(g, 13)
                first_half_out(g, flat(qk[:, ds((i % 2) * 4 + i // 2, 1), :]))

            with act.Fori(0, 4) as i:
                g = i + G_V
                for c in range(6, 12):
                    split_hi(g, c)
                block_out(g, v_flat[:, ds(i * (TM * CB), CB)])
                split_hi(g, 12)
                split_hi(g, 13)

            def exps(pair):
                for t, p in enumerate((p1, p0)):
                    act.wait_ge(max_done, 2 * pair + (t + 1))
                    for h in range(2):
                        last = nc.scalar.activation(p[:, h, :], p[:, h, :], ACT.Exp, bias=neg_max[:, t, h:h + 1],
                                                    accum_out=p_sum[:, t, h:h + 1])
                last.then_inc(exp_done, 1)

            def pT0_out(pair):
                act.wait_ge(pt_done, pair + 1)
                nc.scalar.activation(flat(pT0[:, :, :]), aux[1][:, 0:2 * P], ACT.Copy).then_inc(aux_read[1], 1)

            with act.Fori(0, 4) as i:
                g = i + G_QKA
                split_hi(g, 6)
                split_hi(g, 7)
                exps(i)
                split_hi(g, 8)
                split_hi(g, 9)
                pT0_out(i)
                split_hi(g, 10)
                split_hi(g, 11)
                block_out(g, stage[:, 0, :], 2 * i + 2 * G_V)
                split_hi(g, 12)
                split_hi(g, 13)
                first_half_out(i + G_V, flat(qk[:, ds(2 * i, 1), :]))

            def gate_block(g, i):
                split_hi(g, 6)
                split_hi(g, 7)
                exps(i + 4)
                split_hi(g, 8)
                split_hi(g, 9)
                pT0_out(i + 4)
                split_hi(g, 10)

            def tanh_gate(g, m):
                act.wait_ge(mm_done, g * UNITS + UNITS)
                nc.scalar.activation(t_gate[:, m, :], acc[:, ds((g % 2) * (TM * CB) + m * CB, CB)], ACT.Tanh,
                                     scale=half_rstd[:, m:m + 1]).then_inc(tanh_done, 1)

            with act.Fori(0, 3) as i:
                g = i + G_GATE
                gate_block(g, i)
                split_hi(g, 11)
                for m in range(TM):
                    tanh_gate(g, m)
                split_hi(g, 12)
                split_hi(g, 13)
            gate_block(G_OUT - 1, 3)

            def y_hi(q):
                act.wait_ge(ytr_done, q + 1)
                nc.scalar.activation(flat(a_hi[:, UK * q:UK * q + UK, :]), aux[q % 4][:, :],
                                     ACT.Copy).then_inc(yhi_done, 1)

            act.wait_ge(mm_done, G_OUT * UNITS)
            y_hi(0)
            tanh_gate(G_OUT - 1, 0)
            y_hi(1)
            tanh_gate(G_OUT - 1, 1)
            split_hi(G_OUT, 3)
            y_hi(2)
            y_hi(3)
            for q in range(4, 8):
                y_hi(q)
                split_hi(G_OUT, q)

            nc.scalar.preload_act_table(ACT.Sqrt)

            def square(b, m):
                act.wait_ge(acc_out[m], b + (G_OUT + 1))
                nc.scalar.activation(t_gate[:, m, :], z[:, m, :], ACT.Square,
                                     accum_out=zsq[:, m, ds(b, 1)]).then_inc(zsq_done, 1)

            for c in range(8, 12):
                split_hi(G_OUT, c)
            square(0, 0)
            square(0, 1)
            with act.Fori(1, 3) as b:
                for c in range(4, 12):
                    split_hi(b + G_OUT, c)
                square(b, 0)
                square(b, 1)
            for c in range(4, 8):
                split_hi(G_END - 1, c)
            act.wait_ge(part_var, 1)
            for m in range(TM):
                square(3, m)
                act.wait_ge(zsq_done, 7 + m)
                nc.scalar.activation(zrstd[:, m:m + 1], zsq[:, m, 3:4], ACT.Sqrt, bias=zpart[:, m:m + 1],
                                     scale=1.0 / D).then_inc(fin_std, 1)
            act.wait_ge(fin_rstd, 2)
            act.wait_ge(zg_done, 8)
            nc.scalar.activation(z_gain[:, 1, SCALAR_PART], z_gain[:, 1, SCALAR_PART], ACT.Copy,
                                 scale=zrstd[:, 1:2]).then_inc(scalar_scaled, 1)
            act.wait_ge(scalar_scaled, 1)
            act.dma_start(out[P:2 * P, SCALAR_PART], z_gain[:, 1, SCALAR_PART]).then_inc(out_landed, 16)

        @block.vector
        def _(dve):
            def split_lo(g, c):
                s = c % RING
                dve.wait_ge(hi_done, g * UNITS + (c + 1))
                nc.vector.tensor_tensor(flat(w_lo[:, s, :, :]), w_raw[:, s, :], flat(w_hi[:, s, :, :]).bitcast(f32),
                                        ALU.subtract).then_inc(lo_done, 1)

            def block_out(g, dst, tr=None):
                dve.wait_ge(mm_done, g * UNITS + UNITS)
                if tr is not None:
                    dve.wait_ge(tr_done, tr)
                nc.vector.tensor_scalar(dst, acc[:, ds((g % 2) * (TM * CB) + CB, CB)], rstd[:, 1:2], None,
                                        ALU.mult).then_inc(acc_out[1], 1)

            def second_half_out(tb, dst):
                dve.wait_ge(tr_done, 2 * tb + 2)
                nc.vector.tensor_copy(dst, aux[3][:, :]).then_inc(aux_read[3], 1)

            dve.wait_ge(row_landed, 16)
            last_bias = bias_row[:, 2 * MAX_REL:2 * MAX_REL + 1]
            nc.vector.tensor_copy(bias_ext[:, 0:P - 1], last_bias.broadcast_to((HEADS, P - 1))).then_inc(ext_ready, 1)
            nc.vector.tensor_copy(bias_ext[:, P - 1:3 * P], bias_row[:, ::-1]).then_inc(ext_ready, 1)

            dve.wait_ge(gain_landed, 16)

            def a_part(k):
                dve.wait_ge(ahi_done, k + 1)
                nc.vector.scalar_tensor_tensor(a_lo[:, k, :], xT_land[:, k, :], gain[:, k:k + 1],
                                               a_hi[:, k, :].bitcast(f32), ALU.mult,
                                               ALU.subtract).then_inc(alo_done, 1)

            for u in range(HALVED):
                for kk in range(UK):
                    a_part(u * UK + kk)
                    dve.wait_ge((half_hi, hi_done)[kk], u + 1)
                    nc.vector.tensor_tensor(w_lo[:, u, kk, :], w_raw[:, u, kk * CB:kk * CB + CB],
                                            w_hi[:, u, kk, :].bitcast(f32),
                                            ALU.subtract).then_inc((half_lo, lo_done)[kk], 1)
            for u in range(HALVED, UNITS):
                for k in range(UK * u, UK * u + UK):
                    a_part(k)
                split_lo(0, u)
            nc.vector.memset(iscore1[:, :], 0.0)
            nc.vector.memset(iscore0[:, :], 0.0).then_inc(isum_done, 1)
            dve.wait_ge(patterned, 2)
            nc.vector.scalar_tensor_tensor(dist[:, :], dist[:, :], -1.0, dist[:, :], ALU.mult,
                                           ALU.max).then_inc(pen_step, 1)
            for c in (8, 9, 10):
                split_lo(0, c)
            dve.wait_ge(ssq_done, 1)
            nc.vector.tensor_scalar(ssq[:, :], aux[1][:, 0:TM], 1.0 / D, EPS, ALU.mult, ALU.add).then_inc(var_done, 1)
            dve.wait_ge(std_done, 1)
            nc.vector.reciprocal(rstd[:, :], rstd[:, :]).then_inc(rstd_done, 1)
            dve.wait_ge(rstd_done, 1)
            nc.vector.tensor_scalar(half_rstd[:, :], rstd[:, :], 0.5, None, ALU.mult).then_inc(rstd_done, 1)
            dve.wait_ge(nhi_done, 1)
            nc.vector.tensor_tensor(flat(nw_lo[:, :, :]), nw_raw[:, :], flat(nw_hi[:, :, :]).bitcast(f32),
                                    ALU.subtract).then_inc(nlo_done, 1)
            for c in (11, 12, 13):
                split_lo(0, c)
            block_out(0, stage[:, 1, :])
            split_lo(0, 14)
            split_lo(0, 15)
            second_half_out(0, qiT[:, 1, :])
            split_lo(0, 16)
            split_lo(0, 17)
            dve.wait_ge(narrow_done, 2)
            for m in range(TM):
                for h in range(2):
                    nc.vector.tensor_scalar(ki_nat[:, m, h * IDX_D:(h + 1) * IDX_D],
                                            aux[1][:, m * P:m * P + IDX_D], rstd[:, m:m + 1], None, ALU.mult)
                nc.vector.tensor_scalar(w_idx[:, m, :], aux[1][:, m * P + IDX_D:m * P + NARROW], rstd[:, m:m + 1],
                                        IDX_SCALE, ALU.mult, ALU.mult).then_inc(aux_read[1], 1)
            split_lo(0, 18)
            dve.wait_ge(kit_done, 1)
            dve.wait_ge(cleared, 1)
            nc.vector.tensor_copy(ki_bd[0:IDX_D, 0, :], aux[0][0:IDX_D, 0:T])
            nc.vector.tensor_copy(ki_bd[IDX_D:P, 1, :], aux[0][IDX_D:P, 0:T]).then_inc(aux_read[0], 1)
            split_lo(0, 19)
            block_out(1, stage[:, 1, :], 2)
            dve.wait_ge(khi_done, 1)
            nc.vector.tensor_tensor(ki_lo, flat(ki_bd[:, :, :]), ki_hi.bitcast(f32), ALU.subtract).then_inc(klo_done, 1)
            split_lo(0, 20)
            split_lo(0, 21)
            second_half_out(1, qiT[:, 3, :])

            with dve.Fori(0, 4) as i:
                g = i + G_QB

                def index_sum(c):
                    dve.wait_ge(aux_read[0], 2 * i + (AUX01_INDEX + c + 1))
                    dve.wait_ge(aux_read[1], 2 * i + (AUX01_INDEX + c + 1))
                    dve.wait_ge(isum_done, 2 * i + (c + 1))
                    for h in range(2):
                        for t, (relu, total) in enumerate(((relu1, iscore1), (relu0, iscore0))):
                            if h == 1:
                                dve.wait_ge(isum_step, 4 * i + (2 * c + t + 1))
                            last = nc.vector.scalar_tensor_tensor(
                                total[:, :], relu[:, h, :], w_idx[:, 1 - t, ds(4 * i + (2 * c + h), 1)],
                                total[:, :], ALU.mult, ALU.add)
                            if h == 0:
                                last.then_inc(isum_step, 1)
                    last.then_inc(isum_done, 1)

                split_lo(g, 6)
                split_lo(g, 7)
                index_sum(0)
                split_lo(g, 8)
                split_lo(g, 9)
                index_sum(1)
                split_lo(g, 10)
                split_lo(g, 11)
                block_out(g, stage[:, 1, :], 2 * i + 2 * G_QB)
                split_lo(g, 12)
                split_lo(g, 13)
                second_half_out(g, flat(qk[:, ds((i % 2) * 4 + i // 2 + 2, 1), :]))

            dve.wait_ge(isum_done, 9)
            nc.vector.memset(iscore1[0:HALF, T - CHUNK:T], NOT_ADMITTED).then_inc(top_step, 1)
            nc.vector.memset(iscore0[0:HALF, P - CHUNK:P], NOT_ADMITTED).then_inc(top_step, 1)
            with dve.Fori(0, 4) as i:
                g = i + G_V

                def top_round(r):
                    pairs = ((iscore1, top1), (iscore0, top0))
                    dve.wait_ge(top_step, 8 * i + (4 * r + 2))
                    nc.vector.memset(carrier[:, :], 0.0)
                    for score, top in pairs:
                        nc.vector.max(top[:, :], score[:, :]).then_inc(top_step, 1)
                    dve.wait_ge(top_step, 8 * i + (4 * r + 4))
                    nc.vector.memset(carrier[:, :], 0.0)
                    for score, top in pairs:
                        nc.vector.match_replace(score[:, :], top[:, :], score[:, :], TAKEN).then_inc(top_step, 1)

                split_lo(g, 6)
                split_lo(g, 7)
                top_round(0)
                split_lo(g, 8)
                split_lo(g, 9)
                top_round(1)
                split_lo(g, 10)
                split_lo(g, 11)
                block_out(g, v_flat[:, ds(i * (TM * CB) + CB, CB)])
                split_lo(g, 12)
                split_lo(g, 13)

            dve.wait_ge(top_step, 2 + 4 * (TOP // 8))
            for d, score in ((dist1, iscore1), (dist0, iscore0)):
                nc.vector.tensor_scalar(d[:, :], score[:, :], TAKEN, BIG, ALU.not_equal,
                                        ALU.mult).then_inc(pen_step, 1)
            dve.wait_ge(pen_step, 3)
            nc.vector.tensor_tensor(dist1[:, :], dist1[:, :], dist[:, :], ALU.add).then_inc(pen_step, 1)
            nc.vector.tensor_tensor(dist0[:, :], dist0[:, :], dist[:, P:T], ALU.add).then_inc(pen_step, 1)
            dve.wait_ge(bias_landed, 16)
            nc.vector.memset(bias[0:HALF, :, T - CHUNK:T], MASKED).then_inc(bias_masked, 1)
            dve.wait_ge(bias_masked, 1)
            dve.wait_ge(pen_step, 5)
            dve.wait_ge(cleared, 4 + HEADS)

            def maxima(pair):
                for t, p in enumerate((p1, p0)):
                    if t == 0:
                        dve.wait_ge(aux_read[0], pair + (AUX01_PAIRS + 1))
                    else:
                        dve.wait_ge(biased, pair + 1)
                    nc.vector.tensor_reduce(neg_max[:, t, :], p[:, :, :], AX.X, ALU.max,
                                            negate=True).then_inc(max_done, 1)

            def bias_b(pair):
                dve.wait_ge(scored, pair + 1)
                for t, (p, d, bank, n) in enumerate(((p1, dist1, aux[0], T), (p0, dist0, aux[1], P))):
                    for h in range(2):
                        last = nc.vector.scalar_tensor_tensor(p[:, h, :], d[:, :], neg_slope[:, ds(2 * pair + h, 1)],
                                                              bank[:, h * n:h * n + n], ALU.mult, ALU.add)
                    last.then_inc(aux_read[0] if t == 0 else biased, 1)

            def bias_a(i):
                pair = i + 4
                dve.wait_ge(scored, pair + 1)
                nc.vector.tensor_tensor(p1[:, :, :], aux[0][:, :].rearrange("p (h k) -> p h k", h=2),
                                        bias[:, ds(2 * i, 2), :], ALU.add).then_inc(aux_read[0], 1)
                nc.vector.tensor_tensor(p0[:, :, :], aux[1][:, 0:2 * P].rearrange("p (h k) -> p h k", h=2),
                                        bias[:, ds(2 * i, 2), P:T], ALU.add).then_inc(biased, 1)

            def pT1_out(pair):
                dve.wait_ge(exp_done, pair + 1)
                nc.vector.reciprocal(flat(p_inv[:, :, :]), flat(p_sum[:, :, :])).then_inc(inv_done, 1)
                dve.wait_ge(pt_done, pair + 1)
                nc.vector.tensor_copy(pT1[:, :, :, :].rearrange("p h k q -> p (h k q)"),
                                      aux[2][:, :]).then_inc(aux_read[2], 1)

            def outputs(pair):
                dve.wait_ge(pv_done, pair + 1)
                dve.wait_ge(inv_done, pair + 1)
                for t in range(2):
                    last = nc.vector.tensor_tensor(
                        o_flat[:, ds(place(pair, 1 - t), PAIR)].rearrange("p (h d) -> p h d", h=2),
                        aux[3][:, t * PAIR:t * PAIR + PAIR].rearrange("p (h d) -> p h d", h=2),
                        p_inv[:, t, :].unsqueeze(2).broadcast_to((P, 2, HD)), ALU.mult)
                last.then_inc(aux_read[3], 1)

            with dve.Fori(0, 4) as i:
                g = i + G_QKA
                split_lo(g, 6)
                bias_b(i)
                maxima(i)
                split_lo(g, 7)
                split_lo(g, 8)
                pT1_out(i)
                split_lo(g, 9)
                split_lo(g, 10)
                outputs(i)
                split_lo(g, 11)
                block_out(g, stage[:, 1, :], 2 * i + 2 * G_V)
                split_lo(g, 12)
                split_lo(g, 13)
                second_half_out(i + G_V, flat(qk[:, ds(2 * i + 1, 1), :]))

            def gate_block(g, i):
                split_lo(g, 6)
                bias_a(i)
                maxima(i + 4)
                split_lo(g, 7)
                split_lo(g, 8)
                pT1_out(i + 4)
                split_lo(g, 9)
                split_lo(g, 10)
                outputs(i + 4)

            def gated(g, i, m):
                ob = o_flat[:, ds(i * (TM * CB) + m * CB, CB)]
                dve.wait_ge(tanh_done, 2 * i + (m + 1))
                dve.wait_ge(aux_read[3], i + (AUX23_A + 1))
                nc.vector.scalar_tensor_tensor(ob, acc[:, ds((g % 2) * (TM * CB) + m * CB, CB)],
                                               half_rstd[:, m:m + 1], ob, ALU.mult, ALU.mult).then_inc(acc_out[m], 1)
                dve.wait_ge(acc_out[m], g + 1)
                nc.vector.scalar_tensor_tensor(ob, t_gate[:, m, :], 1.0, ob, ALU.add, ALU.mult).then_inc(y_done, 1)

            with dve.Fori(0, 3) as i:
                g = i + G_GATE
                gate_block(g, i)
                split_lo(g, 11)
                for m in range(TM):
                    gated(g, i, m)
                split_lo(g, 12)
                split_lo(g, 13)

            def y_lo(q):
                dve.wait_ge(yhi_done, q + 1)
                nc.vector.tensor_tensor(flat(a_lo[:, UK * q:UK * q + UK, :]), aux[q % 4][:, :],
                                        flat(a_hi[:, UK * q:UK * q + UK, :]).bitcast(f32),
                                        ALU.subtract).then_inc(ylo_done, 1)

            gate_block(G_OUT - 1, 3)
            y_lo(0)
            gated(G_OUT - 1, 3, 0)
            y_lo(1)
            gated(G_OUT - 1, 3, 1)
            split_lo(G_OUT, 3)
            y_lo(2)
            y_lo(3)
            for q in range(4, 8):
                y_lo(q)
                split_lo(G_OUT, q)

            def residual(g, b, tiles=(0, 1)):
                for m in tiles:
                    nc.vector.tensor_tensor(z[:, m, :], acc[:, ds((g % 2) * (TM * CB) + m * CB, CB)],
                                            v_flat[:, ds(m * D + b * CB, CB)], ALU.add).then_inc(acc_out[m], 1)
                for m in tiles:
                    dve.wait_ge(acc_out[m], g + 1)
                    nc.vector.tensor_tensor(o_flat[:, ds(m * D + b * CB, CB)], z[:, m, :], fgain[:, ds(b * CB, CB)],
                                            ALU.mult).then_inc(zg_done, 1)

            for c in range(8, 12):
                split_lo(G_OUT, c)
            dve.wait_ge(res_landed, 16)
            dve.wait_ge(fgain_landed, 16)
            dve.wait_ge(mm_done, G_OUT * UNITS + UNITS)
            residual(G_OUT, 0)
            with dve.Fori(1, 3) as b:
                for c in range(4, 12):
                    split_lo(b + G_OUT, c)
                dve.wait_ge(zsq_done, 2 * b)
                dve.wait_ge(mm_done, b * UNITS + (G_OUT * UNITS + UNITS))
                residual(b + G_OUT, b)
            for c in range(4, 8):
                split_lo(G_END - 1, c)
            dve.wait_ge(zsq_done, 6)
            nc.vector.tensor_reduce(zpart[:, :], zsq[:, :, 0:3], AX.X, ALU.add).then_inc(part_sum, 1)
            dve.wait_ge(part_sum, 1)
            nc.vector.tensor_scalar(zpart[:, :], zpart[:, :], 1.0 / D, EPS, ALU.mult, ALU.add).then_inc(part_var, 1)
            for m in range(TM):
                dve.wait_ge(tail_done, m + 1)
                residual(G_END - 1, 3, (m,))
                dve.wait_ge(fin_std, m + 1)
                nc.vector.reciprocal(zrstd[:, m:m + 1], zrstd[:, m:m + 1]).then_inc(fin_rstd, 1)
                dve.wait_ge(fin_rstd, m + 1)
                dve.wait_ge(zg_done, 7 + m)
                for part in (part for tile, part in VECTOR_PARTS if tile == m):
                    nc.vector.tensor_scalar(z_gain[:, m, part], z_gain[:, m, part], zrstd[:, m:m + 1], None,
                                            ALU.mult).then_inc(vector_scaled, 1)


_OFFSETS = {"qa": 0, "ka": 1024, "va": 2048, "ga": 3072, "qb": 4096, "kb": 5120, "vb": 6144, "gb": 7168, "qi": 8192}
_STREAM = ["qi", "qb", "kb", "vb", "va", "qa", "ka", "gb", "ga"]


def kernel(x, norm_gain, w_in, rel_bias, w_out, final_gain):
    import numpy as np
    import concourse.bacc as bacc
    from concourse.bass_utils import run_bass_kernel_spmd

    x, w_in, w_out = np.asarray(x)[0], np.asarray(w_in)[0], np.asarray(w_out)[0]

    def units(w):
        return w.reshape(UNITS, UK, P, CB).transpose(0, 2, 1, 3).reshape(UNITS, P, UK * CB)

    starts = [_OFFSETS[name] + half * CB for name in _STREAM for half in range(2)]
    narrow = w_in[:, 9216:9216 + NARROW]
    w_out = np.concatenate([w_out[D // 2:], w_out[:D // 2]])
    arrays = {
        "xT": x.T.reshape(KT, P, T).transpose(1, 0, 2),
        "x": x.reshape(TM, P, D).transpose(1, 0, 2),
        "norm_gain": np.asarray(norm_gain)[0].reshape(KT, P).T,
        "w_blocks": np.stack([units(w_in[:, c:c + CB]) for c in starts]),
        "w_narrow": narrow.reshape(KT, P, NARROW).transpose(1, 0, 2).reshape(P, KT * NARROW),
        "rel_bias": np.asarray(rel_bias)[0],
        "wo_blocks": np.stack([units(w_out[:, c:c + CB]) for c in range(0, D, CB)]),
        "final_gain": np.asarray(final_gain),
    }
    arrays = {name: np.ascontiguousarray(a) for name, a in arrays.items()}
    nc = bacc.Bacc("TRN2", target_bir_lowering=False, num_devices=1)
    args = [nc.dram_tensor(name, a.shape, mybir.dt.from_np(a.dtype), kind="ExternalInput").ap()
            for name, a in arrays.items()]
    out = nc.dram_tensor("out", (T, D), mybir.dt.float32, kind="ExternalOutput").ap()
    hybrid_block(nc, *args, out)
    r = run_bass_kernel_spmd(nc, [arrays], core_ids=[0])
    return r.results[0]["out"].reshape(1, T, D)
```
